# Optimizing a Trainium2 kernel written in Bass

```python
import math
import jax, jax.numpy as jnp
from jax import lax
import numpy as np

D_MODEL = 2048
BATCH = 1
SEQ = 256
DEPTH = 1
DEC_BATCH = 8
DEC_SEQ = 4
PAST_LEN = 256
PAGE_SIZE = 128

HEAD_DIM = 128
N_HEADS_TOTAL = D_MODEL // HEAD_DIM
N_HEADS_B = N_HEADS_TOTAL // 2
N_GROUPS_A = N_HEADS_TOTAL - N_HEADS_B
W_B = N_HEADS_B * HEAD_DIM
W_A = N_GROUPS_A * HEAD_DIM
D_MIX = W_A + W_B
CHUNK = 128
MOBA_BLOCK = 256
MOBA_TOPK = 3
MOBA_GATHER_ROWS = 64
NUM_BUCKETS = 32
MAX_DISTANCE = 1024
CONV_W = 3
D_FF = ((8 * D_MODEL // 3 + 127) // 128) * 128
ALPHA = (2 * DEPTH) ** 0.25
BETA = (8 * DEPTH) ** -0.25
LN_EPS = 1e-5
NEG_INF = -1e30

kernel_name = 'hymba_gmlp_moba_convffn_decoder_step'

def layer_norm(x, g, b):
    xf = x.astype(jnp.float32)
    mu = jnp.mean(xf, axis=-1, keepdims=True)
    var = jnp.mean(jnp.square(xf - mu), axis=-1, keepdims=True)
    return ((xf - mu) * lax.rsqrt(var + LN_EPS) * g.astype(jnp.float32) + b.astype(jnp.float32)).astype(x.dtype)

def rms_norm(x, g):
    xf = x.astype(jnp.float32)
    return (xf * lax.rsqrt(jnp.mean(xf * xf, axis=-1, keepdims=True) + LN_EPS) * g.astype(jnp.float32)).astype(x.dtype)

def t5_bucket(rel):
    n = jnp.maximum(rel, 0)
    max_exact = NUM_BUCKETS // 2
    nf = jnp.maximum(n, 1).astype(jnp.float32)
    large = max_exact + (jnp.log(nf / max_exact) / math.log(MAX_DISTANCE / max_exact)
                         * (NUM_BUCKETS - max_exact)).astype(jnp.int32)
    large = jnp.minimum(large, NUM_BUCKETS - 1)
    return jnp.where(n < max_exact, n, large)

def query_chunk(n, t):
    qc = max(1, MOBA_GATHER_ROWS // n)
    while t % qc:
        qc -= 1
    return qc

def moba_attention(q, k_pad, v_pad, pos0, rel_bias):
    n, t, h, dh = q.shape
    nb = k_pad.shape[1] // MOBA_BLOCK
    k_blk = k_pad.reshape(n, nb, MOBA_BLOCK, h, dh)
    v_blk = v_pad.reshape(n, nb, MOBA_BLOCK, h, dh)
    k_mean = jnp.mean(k_blk.astype(jnp.float32), axis=2)
    topk = min(MOBA_TOPK, nb)
    qc_len = query_chunk(n, t)
    n_chunks = t // qc_len
    qs = (q * HEAD_DIM ** -0.5).reshape(n, n_chunks, qc_len, h, dh).transpose(1, 0, 3, 2, 4)
    pos = (pos0 + jnp.arange(t, dtype=jnp.int32)).reshape(n_chunks, qc_len)
    n_idx = jnp.arange(n)[:, None, None, None]
    h_idx = jnp.arange(h)[None, :, None, None]
    bias_hb = rel_bias.astype(jnp.float32).T
    blk_ids = jnp.arange(nb, dtype=jnp.int32)
    offs = jnp.arange(MOBA_BLOCK, dtype=jnp.int32)

    def attend(args):
        qc, p = args
        q_blk = p // MOBA_BLOCK
        score = jnp.einsum('nhtd,njhd->nhtj', qc.astype(jnp.float32), k_mean)
        fully_past = blk_ids[None, :] < q_blk[:, None]
        score = jnp.where(fully_past, score, NEG_INF)
        _, sel = lax.top_k(score, topk)
        sel_ok = sel < q_blk[:, None]
        own = jnp.broadcast_to(q_blk[:, None], (n, h, qc_len, 1)).astype(sel.dtype)
        blocks = jnp.concatenate([sel, own], axis=-1)
        blk_ok = jnp.concatenate([sel_ok, jnp.ones(own.shape, dtype=bool)], axis=-1)
        kg = k_blk[n_idx, blocks, :, h_idx]
        vg = v_blk[n_idx, blocks, :, h_idx]
        logits = jnp.einsum('nhtd,nhtsbd->nhtsb', qc, kg).astype(jnp.float32)
        rel = p[:, None, None] - (blocks[..., None] * MOBA_BLOCK + offs)
        bias = bias_hb[h_idx[..., None], t5_bucket(rel)]
        ok = blk_ok[..., None] & (rel >= 0)
        logits = jnp.where(ok, logits + bias, NEG_INF)
        shp = logits.shape
        prob = jax.nn.softmax(logits.reshape(shp[:3] + (-1,)), axis=-1).reshape(shp)
        return jnp.einsum('nhtsb,nhtsbd->nhtd', prob.astype(vg.dtype), vg)

    out = lax.map(attend, (qs, pos))
    return out.transpose(1, 0, 3, 2, 4).reshape(n, t, h * dh)

def chunk_spatial_gate(u, v, w_s, b_s):
    n, t, g, c = v.shape
    pad = (-t) % CHUNK
    nc = (t + pad) // CHUNK
    vp = jnp.pad(v, ((0, 0), (0, pad), (0, 0), (0, 0))).reshape(n, nc, CHUNK, g, c)
    w = w_s * jnp.tril(jnp.ones((CHUNK, CHUNK), w_s.dtype))
    mixed = jnp.einsum('gts,ncsgd->nctgd', w, vp) + b_s.T[None, None, :, :, None]
    return u * mixed.reshape(n, nc * CHUNK, g, c)[:, :t]

def decoder_layer(x, c, past_k, past_v, past_up, p):
    n, t, _ = x.shape
    pos0 = past_k.shape[1]
    mod = jnp.dot(jax.nn.silu(c), p['w_ada']) + p['b_ada']
    shift1, scale1, gate1, shift2, scale2, gate2 = jnp.split(mod[:, None, :], 6, axis=-1)
    h = x * (1 + scale1) + shift1
    proj = jnp.dot(h, p['w_in'])
    q, k, v, u_a, v_a = jnp.split(proj, [W_B, 2 * W_B, 3 * W_B, 3 * W_B + W_A], axis=-1)
    heads = (n, t, N_HEADS_B, HEAD_DIM)
    q, k, v = q.reshape(heads), k.reshape(heads), v.reshape(heads)
    pad = (-(pos0 + t)) % MOBA_BLOCK
    tail = jnp.zeros((n, pad, N_HEADS_B, HEAD_DIM), k.dtype)
    k_all = jnp.concatenate([past_k.astype(k.dtype), k, tail], axis=1)
    v_all = jnp.concatenate([past_v.astype(v.dtype), v, tail], axis=1)
    attn = moba_attention(q, k_all, v_all, pos0, p['rel_bias'])
    u_a = jax.nn.gelu(u_a)
    v_a = layer_norm(jax.nn.gelu(v_a), p['ln_sgu_g'], p['ln_sgu_b'])
    groups = (n, t, N_GROUPS_A, HEAD_DIM)
    gm = chunk_spatial_gate(u_a.reshape(groups), v_a.reshape(groups), p['w_s'], p['b_s']).reshape(n, t, W_A)
    mixed = jnp.concatenate([rms_norm(gm, p['norm_a_g']), rms_norm(attn, p['norm_b_g'])], axis=-1)
    x = layer_norm(ALPHA * x + gate1 * jnp.dot(mixed, p['w_out']), p['ln1_g'], p['ln1_b'])
    h = x * (1 + scale2) + shift2
    up = jnp.dot(h, p['w_up'])
    full = jnp.concatenate([past_up.astype(up.dtype), up], axis=1)
    conv = p['b_conv'] + sum(full[:, i:i + t] * p['w_conv'][i] for i in range(CONV_W))
    a, b = jnp.split(conv, 2, axis=-1)
    ff = jnp.dot(jax.nn.silu(a) * b, p['w_down'])
    y = layer_norm(ALPHA * x + gate2 * ff, p['ln2_g'], p['ln2_b'])
    return y, k, v, v_a, full[:, t:]

def setup_inputs(seed: int = 0) -> dict:
    key = jax.random.key(seed)
    ks = jax.random.split(key, 32)
    f32 = jnp.float32
    n_pages = PAST_LEN // PAGE_SIZE
    n_used = DEC_BATCH * n_pages
    n_phys = n_used + max(1, n_used // 4)

    def nrm(k, shape, s):
        return jax.random.normal(k, shape, f32) * s

    page_table = jax.random.permutation(ks[0], n_phys)[:n_used].reshape(DEC_BATCH, n_pages).astype(jnp.int32)
    return {
        'x_prompt': nrm(ks[1], (BATCH, SEQ, D_MODEL), 1.0),
        'x_sample': nrm(ks[2], (DEC_BATCH, DEC_SEQ, D_MODEL), 1.0),
        'cache_k': nrm(ks[3], (DEPTH, n_phys, PAGE_SIZE, N_HEADS_B, HEAD_DIM), 1.0),
        'cache_v': nrm(ks[4], (DEPTH, n_phys, PAGE_SIZE, N_HEADS_B, HEAD_DIM), 1.0),
        'state_ffn_conv': nrm(ks[5], (DEPTH, DEC_BATCH, CONV_W - 1, 2 * D_FF), 1.0),
        'page_table': page_table,
        'c_prompt': nrm(ks[6], (BATCH, D_MODEL), 1.0),
        'c_sample': nrm(ks[7], (DEC_BATCH, D_MODEL), 1.0),
        'w_ada': nrm(ks[8], (DEPTH, D_MODEL, 6 * D_MODEL), 0.5 * D_MODEL ** -0.5),
        'b_ada': nrm(ks[9], (DEPTH, 6 * D_MODEL), 0.02),
        'w_in': nrm(ks[10], (DEPTH, D_MODEL, 3 * W_B + 2 * W_A), D_MODEL ** -0.5),
        'ln_sgu_g': 1.0 + nrm(ks[11], (DEPTH, W_A), 0.1),
        'ln_sgu_b': nrm(ks[12], (DEPTH, W_A), 0.02),
        'w_s': nrm(ks[13], (DEPTH, N_GROUPS_A, CHUNK, CHUNK), CHUNK ** -0.5),
        'b_s': 1.0 + nrm(ks[14], (DEPTH, N_GROUPS_A, CHUNK), 0.1),
        'rel_bias': nrm(ks[15], (NUM_BUCKETS, N_HEADS_B), 0.5),
        'norm_a_g': 1.0 + nrm(ks[16], (DEPTH, W_A), 0.1),
        'norm_b_g': 1.0 + nrm(ks[17], (DEPTH, W_B), 0.1),
        'w_out': nrm(ks[18], (DEPTH, D_MIX, D_MODEL), BETA * D_MIX ** -0.5),
        'ln1_g': 1.0 + nrm(ks[19], (DEPTH, D_MODEL), 0.1),
        'ln1_b': nrm(ks[20], (DEPTH, D_MODEL), 0.02),
        'w_up': nrm(ks[21], (DEPTH, D_MODEL, 2 * D_FF), D_MODEL ** -0.5),
        'w_conv': nrm(ks[22], (DEPTH, CONV_W, 2 * D_FF), CONV_W ** -0.5),
        'b_conv': nrm(ks[23], (DEPTH, 2 * D_FF), 0.02),
        'w_down': nrm(ks[24], (DEPTH, D_FF, D_MODEL), BETA * D_FF ** -0.5),
        'ln2_g': 1.0 + nrm(ks[25], (DEPTH, D_MODEL), 0.1),
        'ln2_b': nrm(ks[26], (DEPTH, D_MODEL), 0.02),
    }

def reference(x_prompt, x_sample, cache_k, cache_v, state_ffn_conv, page_table, c_prompt, c_sample,
              w_ada, b_ada, w_in, ln_sgu_g, ln_sgu_b, w_s, b_s, rel_bias, norm_a_g, norm_b_g, w_out,
              ln1_g, ln1_b, w_up, w_conv, b_conv, w_down, ln2_g, ln2_b):
    bp = x_prompt.shape[0]
    db, n_pages = page_table.shape
    empty = jnp.zeros((bp, 0, N_HEADS_B, HEAD_DIM), x_prompt.dtype)
    up0 = jnp.zeros((bp, CONV_W - 1, 2 * D_FF), x_prompt.dtype)
    y_prompt, y_sample = x_prompt, x_sample
    k_p, v_p, conv_p, k_s, v_s, chunk_v_s, conv_s = [], [], [], [], [], [], []
    for l in range(DEPTH):
        p = {'w_ada': w_ada[l], 'b_ada': b_ada[l], 'w_in': w_in[l], 'ln_sgu_g': ln_sgu_g[l],
             'ln_sgu_b': ln_sgu_b[l], 'w_s': w_s[l], 'b_s': b_s[l], 'rel_bias': rel_bias,
             'norm_a_g': norm_a_g[l], 'norm_b_g': norm_b_g[l], 'w_out': w_out[l], 'ln1_g': ln1_g[l],
             'ln1_b': ln1_b[l], 'w_up': w_up[l], 'w_conv': w_conv[l], 'b_conv': b_conv[l],
             'w_down': w_down[l], 'ln2_g': ln2_g[l], 'ln2_b': ln2_b[l]}
        past_k = cache_k[l][page_table].reshape(db, n_pages * PAGE_SIZE, N_HEADS_B, HEAD_DIM)
        past_v = cache_v[l][page_table].reshape(db, n_pages * PAGE_SIZE, N_HEADS_B, HEAD_DIM)
        y_prompt, kp, vp, _, cp = decoder_layer(y_prompt, c_prompt, empty, empty, up0, p)
        y_sample, ks_, vs_, chv, cs = decoder_layer(y_sample, c_sample, past_k, past_v, state_ffn_conv[l], p)
        k_p.append(kp); v_p.append(vp); conv_p.append(cp)
        k_s.append(ks_); v_s.append(vs_); chunk_v_s.append(chv); conv_s.append(cs)
    return (y_prompt, y_sample, jnp.stack(k_p), jnp.stack(v_p), jnp.stack(conv_p),
            jnp.stack(k_s), jnp.stack(v_s), jnp.stack(chunk_v_s), jnp.stack(conv_s))


_drawn_inputs = setup_inputs


def setup_inputs(seed=0):
    import zlib

    import numpy as np

    out = dict(_drawn_inputs(seed))
    spreads = {}
    factors = {'ln_sgu_b': 2.905,
     'b_s': 6.115,
     'norm_a_g': 5.522,
     'norm_b_g': 5.584,
     'ln1_b': 2.878,
     'b_conv': 8.0,
     'ln2_b': 2.907}
    for name, (base, spread) in spreads.items():
        noise = np.random.default_rng([zlib.crc32(name.encode()), seed]).standard_normal(out[name].shape)
        drawn = base * np.exp(spread * noise) if base else spread * noise
        out[name] = __import__('jax').numpy.asarray(drawn.astype(out[name].dtype))
    for name, factor in factors.items():
        out[name] = (out[name] * factor).astype(out[name].dtype)
    return out
```

```python
import math
from contextlib import ExitStack

import concourse.bass as bass
import numpy as np
from concourse import mybir

F32 = mybir.dt.float32
F32R = mybir.dt.float32r
I32 = mybir.dt.int32
ALU = mybir.AluOpType
ACT = mybir.ActivationFunctionType
AX = mybir.AxisListType

P = 128
D = 2048
SEQ = 256
NSEQ, TOK = 8, 4
SAMP = NSEQ * TOK
ROWS = SEQ + SAMP
HEADS = 8
PAST = 256
PAGES = 2
FF = 5504
KT = D // P
FT = FF // P
BUCKETS, MAXDIST = 32, 1024
ALPHA = 2.0 ** 0.25
EPS = 1e-5
NEG = -1e30
SCALE = float(P) ** -0.5
UW = SEQ + 2 + NSEQ * (TOK + 2)
CW = UW - 2
TABLES = 1 + 4 * TOK
MODS = 9

SLAB = 2 * 4 * P
RING = 4
AHEAD = 3
IN_GROUPS, IN_STEPS = 10, 20
PHASE_K = [16, 16, 11]
UP_GROUPS = [8, 8, 5]
S_IN = 0
S_OUT = S_IN + 4 * IN_STEPS
S_UP = [S_OUT + 32, S_OUT + 128, S_OUT + 224]
S_DN = [S_UP[0] + 64, S_UP[1] + 64, S_UP[2] + 48]
S_END = S_DN[2] + 24

TD_IN, TD_OUT = 0, 3 * 40
TD_UP = [3 * 44, 3 * 56, 3 * 68]
TD_DN = [3 * 52, 3 * 64, 3 * 73 + 1]
GROUPS_BEFORE = [0, 8, 16]

ADA_STEPS = 16
G1, SH2, SC2, G2 = 32, 48, 64, 80

V_ADA, V_G1, V_B1, V_NA, V_NB, V_G2, V_B2, V_CONV = 0, 96, 112, 128, 136, 144, 160, 176
V_ALL = V_CONV + 4 * 2 * FT
C_ID, C_TRI, C_M32, C_MP, C_MN, C_BD = 0, 128, 256, 512, 544, 576
C_ALL = 608
REL_MAX = PAST + TOK - 1
REL_N = REL_MAX + 1 + 127


def buckets(n):
    nf = np.maximum(n, 1).astype(np.float32)
    half = BUCKETS // 2
    large = half + (np.log(nf / np.float32(half)) / np.float32(math.log(MAXDIST / half)) * np.float32(half)).astype(np.int32)
    return np.where(n < half, n, np.minimum(large, BUCKETS - 1))


def shape_constants():
    c = np.zeros((P, C_ALL), np.float32)
    i = np.arange(P)
    c[:, C_ID:C_ID + P] = np.eye(P)
    c[:, C_TRI:C_TRI + P] = i[None, :] >= i[:, None]
    own = (np.arange(SAMP)[None, :] // TOK == np.arange(NSEQ)[:, None]).astype(np.float32)
    c[:, C_M32:C_M32 + NSEQ * SAMP] = own.reshape(1, -1)
    mine = (i[:, None] % SAMP) // TOK == np.arange(SAMP)[None, :] // TOK
    c[:, C_MP:C_MP + SAMP] = mine
    c[:, C_MN:C_MN + SAMP] = np.where(mine, 0.0, NEG)
    j = np.arange(SAMP)
    c[:SAMP, C_BD:C_BD + SAMP] = j[None, :] % TOK >= j[:, None] % TOK
    rel = REL_MAX - np.arange(REL_N)
    hot = np.zeros((BUCKETS + 1, REL_N), np.float32)
    hot[np.where(rel >= 0, buckets(np.maximum(rel, 0)), BUCKETS), np.arange(REL_N)] = 1.0
    return c, hot




SBUF_BYTES = 212000


class Steps:

    def __init__(self, eng, sem):
        self.eng, self.sem, self.n, self.it, self.per, self.start = eng, sem, 0, None, 0, 0

    def link(self, ins):
        self.n += 1
        ins.then_inc(self.sem, 1)
        self.eng.wait_ge(self.sem, self.n if self.it is None else self.it * self.per + self.n)

    def enter(self, it, per):
        self.it, self.per, self.start = it, per, self.n

    def leave(self, iterations):
        assert self.n - self.start == self.per, (self.n - self.start, self.per)
        self.n += self.per * (iterations - 1)
        self.it = None


def decoder_layer_program(nc, io, n_phys):
    with ExitStack() as ctx:
        base = (nc.sbuf_base + 31) // 32 * 32
        ctx.enter_context(nc.sbuf_tensor("arena", [P, SBUF_BYTES // 4], F32))
        top = 0

        def place(name, shape, dt=F32, over=None):
            nonlocal top
            size = (4 * int(np.prod(shape[1:])) + 31) // 32 * 32
            offset = top if over is None else over
            if over is None:
                top += size
            assert offset + size <= SBUF_BYTES - 32, (name, offset + size)
            return nc.alloc_sbuf_tensor_at(name, shape, dt, offset=base + offset), offset

        T = KT * ROWS
        xT, _ = place("xT", [P, T])
        hH, o_h = place("hH", [P, T], F32R)
        hL, _ = place("hL", [P, T], F32R)
        modT, _ = place("modT", [P, 96 * MODS])
        vec, _ = place("vec", [P, V_ALL])
        cst, _ = place("cst", [P, C_ALL])
        ones, _ = place("ones", [P, P])
        cT, _ = place("cT", [P, KT * 32])
        raw, _ = place("raw", [P, RING * SLAB])
        wH, _ = place("wH", [P, RING * SLAB], F32R)
        wL, _ = place("wL", [P, RING * SLAB], F32R)
        ada, _ = place("ada", [P, RING * 1024])
        adaS, _ = place("adaS", [P, 256])
        past, _ = place("past", [P, 2 * FT * 16])
        wsT, o_ws = place("wsT", [P, HEADS * P])
        bd, o_bd = place("bd", [SAMP, HEADS * SAMP])
        small, _ = place("small", [P, 160])
        cw, _ = place("cw", [P, 16])
        pages, _ = place("pages", [1, 16], I32)
        region = top
        proj, o_proj = place("proj", [P, 40 * ROWS])
        o_va = o_proj + 4 * 32 * ROWS
        Vrm, o_v = place("Vrm", [P, 2 * 1024])
        Vn, o_vn = place("Vn", [SAMP, 1024])
        VAs, _ = place("VAs", [SAMP, 1024])
        H32, _ = place("H32", [P, 4 * ROWS], over=o_v)
        hot, _ = place("hot", [BUCKETS + 1, REL_N], over=o_vn)
        rbias, _ = place("rbias", [BUCKETS + 1, HEADS], over=o_vn + 1568)
        bvec, _ = place("bvec", [HEADS, 2 * REL_N], over=o_vn + 1632)
        RR, _ = place("RR", [P, 2 * ROWS], over=o_v)
        Tm, _ = place("Tm", [P, 2 * 512], over=o_va)
        Lp, _ = place("Lp", [P, 2 * 384], over=o_va)
        Pp, _ = place("Pp", [P, 2 * 384], over=o_va + 3072)
        PTp, _ = place("PTp", [P, 2 * 384], over=o_va + 6144)
        VA, _ = place("VA", [P, 2 * 1024], over=o_h)
        BS, _ = place("BS", [P, 1024], over=o_h + 8192)
        SG, _ = place("SG", [P, 1024], over=o_h + 12288)
        SH, _ = place("SH", [P, 1024], over=o_h + 16384)
        KV, _ = place("KV", [P, 2 * 2048], over=o_h + 20480)
        TB, _ = place("TB", [P, HEADS * 256], over=o_h)
        SBi, _ = place("SBi", [P, 2 * ROWS], over=o_h + 8192)
        Ls, _ = place("Ls", [P, 2 * ROWS], over=o_h + 10496)
        PTs, _ = place("PTs", [P, 4 * P], over=o_h + 12800)
        PN, _ = place("PN", [SAMP, 2 * P], over=o_h + 14848)
        Qm, _ = place("Qm", [P, 2 * 256], over=o_h + 15872)
        E4, _ = place("E4", [P, 2 * TOK], over=o_h + 17920)
        PTm, _ = place("PTm", [P, 2 * 512], over=o_ws)
        OS, _ = place("OS", [P, 2 * P], over=o_bd)
        top = region
        ffH, _ = place("ffH", [P, 16 * ROWS], F32R)
        ffL, _ = place("ffL", [P, 16 * ROWS], F32R)
        U, _ = place("U", [P, 4 * UW])
        CV, o_cv = place("CV", [P, 4 * CW])
        SA, o_sa = place("SA", [P, 2 * CW])
        Ff, _ = place("Ff", [P, 2 * ROWS])
        E, _ = place("E", [P, 2 * FT * 18])
        S4, o_s4 = place("S4", [P, 4 * ROWS])
        RN, _ = place("RN", [P, 2 * ROWS], over=o_s4)
        DG, _ = place("DG", [P, 6 * P], over=o_cv)
        H2, _ = place("H2", [P, 4 * ROWS], over=o_sa)

        ps = ctx.enter_context(nc.psum_tensor("ps", [P, 8, 512], F32))
        bias_rows = nc.dram_tensor("bias_rows", [2 * HEADS, REL_N], F32, kind="Internal").ap()
        ident = cst[:, C_ID:C_ID + P]

        def sem(name):
            return ctx.enter_context(nc.semaphore(name))

        raw_in = [sem(f"raw_in{i}") for i in range(RING)]
        ada_in = [sem(f"ada_in{i}") for i in range(RING)]
        hi_done = sem("hi_done")
        split_done = sem("split_done")
        used = sem("used")
        tile_done = sem("tile_done")
        ada_used = sem("ada_used")
        bank_full = [sem(f"bank_full{i}") for i in range(8)]
        bank_free = [sem(f"bank_free{i}") for i in range(8)]
        dve_step = sem("dve_step")
        small_in, bias_in, x_in, c_in = sem("small_in"), sem("bias_in"), sem("x_in"), sem("c_in")
        c_silu, proj_zeroed = sem("c_silu"), sem("proj_zeroed")
        adaS_ready = sem("adaS_ready")
        h32_ready, hH_ready, h_ready = sem("h32_ready"), sem("hH_ready"), sem("h_ready")
        proj_ready, gelu_ready = sem("proj_ready"), sem("gelu_ready")
        bvec_stored = sem("bvec_stored")
        sgu_in, table_in = sem("sgu_in"), sem("table_in")
        var_ready, va_sd, va_ready, gm_ready = sem("var_ready"), sem("va_sd"), sem("va_ready"), sem("gm_ready")
        logit_ready, exp_ready, prob_ready = sem("logit_ready"), sem("exp_ready"), sem("prob_ready")
        kv_in, kv_used = [sem("kv_in0"), sem("kv_in1")], sem("kv_used")
        qm_ready, ptm_ready, pages_in, tails_stored = sem("qm_ready"), sem("ptm_ready"), sem("pages_in"), sem("tails_stored")
        s_logit, s_exp, s_prob = sem("s_logit"), sem("s_exp"), sem("s_prob")
        sq_ready, sd_ready, m_ready, mH_ready, m_split = (
            sem("sq_ready"), sem("sd_ready"), sem("m_ready"), sem("mH_ready"), sem("m_split"))
        s4_ready, s4_copied = sem("s4_ready"), sem("s4_copied")
        ln_var, ln_sd, diag_ready = sem("ln_var"), sem("ln_sd"), sem("diag_ready")
        xn_ready, x1_ready = sem("xn_ready"), sem("x1_ready")
        h2_32, h2H, h2_ready = sem("h2_32"), sem("h2H"), sem("h2_ready")
        pads_set, past_ready, tails_ready = sem("pads_set"), sem("past_ready"), sem("tails_ready")
        conv_ready, silu_ready, ff32_ready, ffH_ready, ff_ready = (
            sem("conv_ready"), sem("silu_ready"), sem("ff32_ready"), sem("ffH_ready"), sem("ff_ready"))
        kv_stored, va_stored, stored = sem("kv_stored"), sem("va_stored"), sem("stored")

        taken, done = [1] * 5 + [0] * 3, [0] * 8
        JOBS = {}

        def take(pe, job, bank, it=0, per=0):
            if taken[bank]:
                pe.wait_ge(bank_free[bank], taken[bank] + it * per)
            JOBS[job] = (bank, done[bank], taken[bank], per)
            taken[bank] += 1
            return ps[:, bank, :]

        def fill(ins, job):
            done[JOBS[job][0]] += 1
            ins.then_inc(bank_full[JOBS[job][0]], 1)

        def filled(eng, job, it=0):
            bank, n, _, per = JOBS[job]
            eng.wait_ge(bank_full[bank], n + 1 + it * per)
            return ps[:, bank, :]

        def release(ins, job):
            ins.then_inc(bank_free[JOBS[job][0]], 1)

        def released(eng, job, it=0):
            bank, _, n, per = JOBS[job]
            eng.wait_ge(bank_free[bank], n + 1 + it * per)

        def tile(t, k, lo=0, hi=ROWS):
            return t[:, k * ROWS + lo:k * ROWS + hi]

        def tiles(t, k, n, lo=0, hi=ROWS):
            if isinstance(k, int):
                v = t[:, k * ROWS:(k + n) * ROWS]
            else:
                v = t[:, bass.ds(k * ROWS, n * ROWS)]
            return v.rearrange("p (k c) -> p k c", k=n)[:, :, lo:hi]

        def spread(ap, *dims):
            return bass.AP(ap.tensor, ap.offset, [list(ap.ap[0])] + [list(d) for d in dims])

        def mods(k, n):
            if isinstance(k, int):
                v = modT[:, k * MODS:(k + n) * MODS]
            else:
                v = modT[:, bass.ds(k * MODS, n * MODS)]
            return (spread(v, [MODS, n], [0, SEQ]),
                    spread(v.rearrange("p (k c) -> p k c", k=n)[:, :, 1:MODS], [MODS, n], [1, NSEQ], [0, TOK]))

        def by_seq(v, n):
            return v.rearrange("p k (n t) -> p k n t", t=TOK)

        block = ctx.enter_context(nc.Block())

        @block.tensor
        def _(pe):
            def products(s, i, rhs_hi, rhs_lo, banks, first, last, ktiles=2):
                pe.wait_ge(split_done, s + 1)
                n = len(banks)
                for kk in range(ktiles):
                    for t in range(n):
                        w = (i % RING) * SLAB + (kk * n + t) * P
                        start, stop = first and kk == 0, last and kk == ktiles - 1
                        out = ps[:, banks[t], 0:ROWS]
                        nc.tensor.matmul(out, wH[:, w:w + P], rhs_lo(kk), start=start, stop=False)
                        nc.tensor.matmul(out, wL[:, w:w + P], rhs_hi(kk), start=False, stop=False)
                        mm = nc.tensor.matmul(out, wH[:, w:w + P], rhs_hi(kk), start=False, stop=stop)
                        if kk == ktiles - 1 and t == n - 1:
                            mm.then_inc(used, 1)
                        elif stop:
                            mm.then_inc(tile_done, 1)

            def ada_slab(unit, k):
                if k == 0:
                    if not isinstance(unit, int) or unit > 0:
                        pe.wait_ge(adaS_ready, unit)
                pe.wait_ge(ada_in[k % RING], unit * 64 + 16 * (k // RING + 1))
                for c in range(4):
                    o = (k % RING) * 1024 + 256 * c
                    mm = nc.tensor.matmul(ps[32 * c:32 * c + 32, 6, 0:256], cT[:, 32 * k:32 * k + 32],
                                          ada[:, o:o + 256], start=(k == 0), stop=(k == ADA_STEPS - 1))
                mm.then_inc(ada_used, 1)

            def ada_turn(unit, job, it=0, per=0):
                pe.wait_ge(adaS_ready, unit + 1)
                b = take(pe, job, 7, it, per)
                nc.tensor.transpose(b[:, 0:P], adaS[:, 0:P], ident)
                fill(nc.tensor.transpose(b[:, P:2 * P], adaS[:, P:2 * P], ident), job)

            pe.wait_ge(small_in, 16 * 5)
            pe.wait_ge(bias_in, 32)
            b = take(pe, "bias", 5)
            fill(nc.tensor.matmul(b[0:HEADS, 0:REL_N], rbias[:, :], hot[:, :], start=True, stop=True), "bias")
            pe.wait_ge(c_silu, 1)
            for k in range(ADA_STEPS):
                ada_slab(0, k)
            ada_turn(0, ("turn", 0))

            def w_in_quarter(kg, it, loop):
                pe.wait_ge(h_ready, kg + 1)
                for i in range(IN_STEPS):
                    g, half = divmod(i, 2)
                    banks = [(4 * g + t) % 5 for t in range(4)]
                    if half == 0:
                        for t in range(4):
                            take(pe, ("in", loop, 4 * g + t), banks[t], it, 8)

                    def rhs(src):
                        def at(kk):
                            if loop:
                                return src[:, bass.ds((kg * 4 + 2 * half + kk) * ROWS, ROWS)]
                            return tile(src, kg * 4 + 2 * half + kk)
                        return at
                    products(kg * IN_STEPS + i, i, rhs(hH), rhs(hL), banks, half == 0, half == 1)
                    if i < ADA_STEPS:
                        ada_slab(kg + 1, i)
                    if i == ADA_STEPS:
                        ada_turn(kg + 1, ("turn in", loop), it, 1)

            with pe.Fori(0, 3) as kg:
                w_in_quarter(kg, kg, True)
            for bank in range(5):
                taken[bank] += 2 * 8
            taken[7] += 2
            done[7] += 2
            w_in_quarter(3, 0, False)

            slabs = iter([(u, k) for u in range(5, 10) for k in range(ADA_STEPS)])

            def ada_slabs(n):
                for _ in range(n):
                    ada_slab(*next(slabs))

            pe.wait_ge(proj_ready, 1)
            for hg in range(2):
                for r in range(3):
                    job, n = ("v", r, hg), P if r < 2 else SAMP
                    b = take(pe, job, 3 * hg + r)
                    for h in range(4):
                        mm = nc.tensor.transpose(b[0:n, h * P:(h + 1) * P], tile(proj, 16 + 4 * hg + h, r * P, r * P + n), ident)
                    fill(mm, job)
                    ada_slabs(1)
            pe.wait_ge(gelu_ready, 1)
            for r in range(3):
                for hg in range(2):
                    job, n = ("va", r, hg), P if r < 2 else SAMP
                    b = take(pe, job, 3 * hg + r)
                    for h in range(4):
                        mm = nc.tensor.transpose(b[0:n, h * P:(h + 1) * P], tile(proj, 32 + 4 * hg + h, r * P, r * P + n), ident)
                    fill(mm, job)
                    ada_slabs(1)
            ada_slabs(4)
            ada_turn(5, ("turn", 5))
            for c in range(2):
                pe.wait_ge(va_ready, c + 1)
                for gg in range(2):
                    job = ("gate", c, gg)
                    b = take(pe, job, 2 * c + gg)
                    for g in range(4 * gg, 4 * gg + 4):
                        mm = nc.tensor.matmul(b[:, (g % 4) * P:(g % 4 + 1) * P], VA[:, c * 1024 + g * P:c * 1024 + (g + 1) * P],
                                              wsT[:, g * P:(g + 1) * P], start=True, stop=True)
                    fill(mm, job)
                    ada_slabs(2)
            pe.wait_ge(va_ready, 3)
            b = take(pe, "gate decode", 4)
            for g in range(HEADS):
                mm = nc.tensor.matmul(b[:, g * SAMP:(g + 1) * SAMP], VAs[0:SAMP, g * P:(g + 1) * P],
                                      bd[0:SAMP, g * SAMP:(g + 1) * SAMP], start=True, stop=True)
            fill(mm, "gate decode")
            ada_slabs(8)
            ada_turn(6, ("turn", 6))

            def scores(h):
                b = take(pe, ("S", h), h % 2)
                q, k = lambda lo, hi: tile(proj, h, lo, hi), lambda lo, hi: tile(proj, 8 + h, lo, hi)
                nc.tensor.matmul(b[:, 0:P], q(0, P), k(0, P), start=True, stop=True)
                fill(nc.tensor.matmul(b[:, P:3 * P], q(P, 2 * P), k(0, 2 * P), start=True, stop=True), ("S", h))

            scores(0)
            for h in range(HEADS):
                if h + 1 < HEADS:
                    scores(h + 1)
                ada_slabs(2)
                pe.wait_ge(prob_ready, h + 1)
                b = take(pe, ("PT", h), 2 + h % 2)
                for j in range(3):
                    o = (h % 2) * 384 + j * P
                    mm = nc.tensor.transpose(b[:, j * P:(j + 1) * P], Pp[:, o:o + P], ident)
                fill(mm, ("PT", h))
                b = take(pe, ("PV", h), 4 + h % 2)
                released(pe, ("PT", h))
                o = (h % 2) * 384
                nc.tensor.matmul(b[:, 0:2 * P], Vrm[:, h * P:(h + 1) * P], PTp[:, o:o + 2 * P], start=True, stop=False)
                fill(nc.tensor.matmul(b[:, P:2 * P], Vrm[:, 1024 + h * P:1024 + (h + 1) * P], PTp[:, o + 2 * P:o + 3 * P],
                                      start=False, stop=True), ("PV", h))
            ada_turn(7, ("turn", 7))

            b = take(pe, "S new", 3)
            for h in range(HEADS):
                hh, hq = divmod(h, 4)
                mm = nc.tensor.matmul(b[32 * hq:32 * hq + 32, hh * SAMP:(hh + 1) * SAMP], tile(proj, h, SEQ, ROWS),
                                      tile(proj, 8 + h, SEQ, ROWS), start=True, stop=True)
            fill(mm, "S new")
            take(pe, "S past 0", 0)
            take(pe, "S past 1", 1)
            for n in range(NSEQ):
                pe.wait_ge(kv_in[n % 2], 32 * (n // 2 + 1))
                pe.wait_ge(qm_ready, n + 1)
                for h in range(HEADS):
                    hh, hq = divmod(h, 4)
                    keys = KV[:, (n % 2) * 2048:(n % 2 + 1) * 2048].rearrange("p (g h c) -> p g h c", g=PAGES, h=HEADS)[:, :, h, :]
                    mm = nc.tensor.matmul(ps[32 * hq:32 * hq + 32, hh, 0:PAST], Qm[:, (n % 2) * 256 + h * 32:(n % 2) * 256 + (h + 1) * 32],
                                          keys, start=(n == 0), stop=(n == NSEQ - 1))
                mm.then_inc(kv_used, 1)
                ada_slabs(2)
            ada_turn(8, ("turn", 8))
            pe.wait_ge(s_prob, 1)
            b = take(pe, "s PT", 4)
            for hh in range(2):
                for kt in range(2):
                    mm = nc.tensor.transpose(b[:, (2 * hh + kt) * P:(2 * hh + kt + 1) * P], Ls[:, hh * ROWS + kt * P:hh * ROWS + (kt + 1) * P], ident)
            fill(mm, "s PT")
            b = take(pe, "s PN", 5)
            for hh in range(2):
                mm = nc.tensor.transpose(b[0:SAMP, hh * P:(hh + 1) * P], Ls[:, hh * ROWS + PAST:(hh + 1) * ROWS], ident)
            fill(mm, "s PN")
            take(pe, "O 0", 0)
            take(pe, "O 1", 1)
            for n in range(NSEQ):
                pe.wait_ge(kv_in[n % 2], 32 * (4 + n // 2 + 1))
                pe.wait_ge(ptm_ready, n + 1)
                for kt in range(2):
                    for h in range(HEADS):
                        hh, hq = divmod(h, 4)
                        o = (n % 2) * 512 + ((2 * hh + kt) * 4 + hq) * 32
                        mm = nc.tensor.matmul(ps[32 * hq:32 * hq + 32, hh, 0:P], PTm[:, o:o + 32],
                                              KV[:, (n % 2) * 2048 + kt * 1024 + h * P:(n % 2) * 2048 + kt * 1024 + (h + 1) * P],
                                              start=(n == 0 and kt == 0), stop=False)
                mm.then_inc(kv_used, 1)
                ada_slabs(2)
            released(pe, "s PN")
            for h in range(HEADS):
                hh, hq = divmod(h, 4)
                mm = nc.tensor.matmul(ps[32 * hq:32 * hq + 32, hh, 0:P], PN[0:SAMP, hh * P + 32 * hq:hh * P + 32 * hq + 32],
                                      Vn[0:SAMP, h * P:(h + 1) * P], start=False, stop=True)
                if h == 3:
                    fill(mm, "O 0")
            fill(mm, "O 1")
            released(pe, "O 0")
            released(pe, "O 1")
            b = take(pe, "OT", 2)
            nc.tensor.transpose(b[:, 0:P], OS[:, 0:P], ident)
            fill(nc.tensor.transpose(b[:, P:2 * P], OS[:, P:2 * P], ident), "OT")
            ada_turn(9, ("turn", 9))
            for a, (job, k0) in enumerate((("sum a", 16), ("sum b", 8))):
                pe.wait_ge(sq_ready, a + 1)
                b = take(pe, job, 3 + a)
                for k in range(8):
                    mm = nc.tensor.matmul(b[:, 0:ROWS], ones[:, :], tile(proj, k0 + k), start=(k == 0), stop=(k == 7))
                fill(mm, job)

            def turn_rows(g, ln):
                pe.wait_ge(s4_ready, 4 * ln + g + 1)
                for r, bank in enumerate((4, 5, 7)):
                    n = P if r < 2 else SAMP
                    b = take(pe, ("rows", ln, g, r), bank)
                    for t in range(4):
                        mm = nc.tensor.transpose(b[0:n, t * P:(t + 1) * P], tile(S4, t, r * P, r * P + n), ident)
                    fill(mm, ("rows", ln, g, r))

            def spread_rows(ln):
                pe.wait_ge(diag_ready, ln + 1)
                for j in range(2):
                    b = take(pe, ("ln", ln, j), 4 + j)
                    for r in range(3):
                        n = P if r < 2 else SAMP
                        mm = nc.tensor.matmul(b[:, r * P:r * P + n], ones[0:n, :], DG[0:n, (2 * r + j) * P:(2 * r + j) * P + n],
                                              start=True, stop=True)
                    fill(mm, ("ln", ln, j))

            for g in range(4):
                for j in range(8):
                    if j == 0:
                        for t in range(4):
                            take(pe, ("out", g, t), t)
                    if g == 0:
                        pe.wait_ge(m_split, 2 * j + 2)
                    products(S_OUT + 8 * g + j, j, lambda kk: tile(hH, 2 * j + kk), lambda kk: tile(hL, 2 * j + kk),
                             range(4), j == 0, j == 7)
                    if g and j == 2:
                        turn_rows(g - 1, 0)
            turn_rows(3, 0)
            spread_rows(0)

            def up_group(s, i0, job, it, per, halves=2, units=None):
                banks = [0, 1, 2, 3] if halves == 2 else [0, 2]
                for j in range(8):
                    if j == 0:
                        for t in banks:
                            take(pe, (job, t), t, it, per)
                    pe.wait_ge(h2_ready, j // 2 + 1)
                    products(s + j, i0 + j, lambda kk: tile(hH, 2 * j + kk), lambda kk: tile(hL, 2 * j + kk),
                             banks, j == 0, j == 7)
                    if units is not None:
                        ada_slab(units, i0 + j)

            def after_loop(banks, per, iterations):
                for bank in banks:
                    taken[bank] += per * (iterations - 1)

            for ph in range(3):
                if ph == 0:
                    with pe.Fori(0, 2) as u:
                        up_group(u * 16 + S_UP[0], 0, ("up", 0, "a"), u, 2, units=u + 10)
                        up_group(u * 16 + S_UP[0] + 8, 8, ("up", 0, "b"), u, 2, units=u + 10)
                        ada_turn(u + 10, ("turn up",), u, 1)
                    after_loop(range(4), 2, 2)
                    after_loop([7], 1, 2)
                    done[7] += 1
                    with pe.Fori(0, 4) as g:
                        up_group(g * 8 + S_UP[0] + 32, 0, ("up", 0, "c"), g, 1)
                    after_loop(range(4), 1, 4)
                else:
                    with pe.Fori(0, UP_GROUPS[ph]) as g:
                        up_group(g * 8 + S_UP[ph], 0, ("up", ph), g, 1)
                    after_loop(range(4), 1, UP_GROUPS[ph])
                if ph == 2:
                    up_group(S_UP[2] + 40, 0, ("up tail",), 0, 0, halves=1)
                if ph < 2:
                    with pe.Fori(0, 4) as g:
                        for j in range(8):
                            if j == 0:
                                for t in range(4):
                                    take(pe, ("down", ph, t), t, g, 1)
                            pe.wait_ge(ff_ready, GROUPS_BEFORE[ph] + j + 1)
                            products(g * 8 + S_DN[ph] + j, j, lambda kk: tile(ffH, 2 * j + kk), lambda kk: tile(ffL, 2 * j + kk),
                                     range(4), j == 0, j == 7)
                    after_loop(range(4), 1, 4)
                else:
                    for g in range(4):
                        for j in range(6):
                            if j == 0:
                                for t in range(4):
                                    take(pe, ("down", 2, g, t), t)
                            if g == 0:
                                pe.wait_ge(ff_ready, GROUPS_BEFORE[2] + j + 1)
                            products(S_DN[2] + 6 * g + j, 6 * g + j, lambda kk: tile(ffH, 2 * j + kk),
                                     lambda kk: tile(ffL, 2 * j + kk), range(4), j == 0, j == 5, ktiles=2 if j < 5 else 1)
                            if g and j == 2:
                                turn_rows(g - 1, 1)
                    turn_rows(3, 1)
                    spread_rows(1)

        @block.sync
        def _(sp):
            def load(s, source, index, slot, cols=SLAB):
                if not isinstance(s, int) or s >= RING:
                    sp.wait_ge(split_done, s - RING + 1)
                src = source[bass.ds(index, 1), :, :].rearrange("a p c -> (a p) c") if not isinstance(index, int) else source[index, :, :]
                sp.dma_start(raw[:, slot * SLAB:slot * SLAB + cols], src).then_inc(raw_in[slot], 16)

            def load_ada(unit, k):
                a = unit * ADA_STEPS + k
                if not isinstance(a, int) or a >= RING:
                    sp.wait_ge(ada_used, a - RING + 1)
                src = io["w_ada"][bass.ds(a, 1), :, :].rearrange("a p c -> (a p) c") if not isinstance(a, int) else io["w_ada"][a, :, :]
                sp.dma_start(ada[:, (k % RING) * 1024:(k % RING + 1) * 1024], src).then_inc(ada_in[k % RING], 16)

            for k in range(ADA_STEPS):
                if k >= 13:
                    load(k - 13, io["w_in"], k - 13, k - 13)
                load_ada(0, k)
            load(AHEAD, io["w_in"], AHEAD, AHEAD)
            with sp.Fori(0, 3) as kg:
                for i in range(1, IN_STEPS + 1):
                    if i <= ADA_STEPS:
                        load_ada(kg + 1, i - 1)
                    s = kg * IN_STEPS + (i + AHEAD)
                    load(s, io["w_in"], s, (i + AHEAD) % RING)
            for i in range(1, IN_STEPS + 1):
                if i <= ADA_STEPS:
                    load_ada(4, i - 1)
                s = 3 * IN_STEPS + i + AHEAD
                if s < S_OUT:
                    load(s, io["w_in"], s, s % RING)
                else:
                    load(s, io["w_out"], s - S_OUT, s % RING)
            for u in range(5, 10):
                for k in range(ADA_STEPS):
                    load_ada(u, k)
            for s in range(S_OUT + 4, S_UP[0]):
                load(s, io["w_out"], s - S_OUT, s % RING)
            for j in range(3):
                load(S_UP[0] + j, io["w_up"], j, j)
            with sp.Fori(0, 2) as u:
                for i in range(16):
                    load(u * 16 + (S_UP[0] + i + AHEAD), io["w_up"], u * 16 + (i + AHEAD), (i + AHEAD) % RING)
                    load_ada(u + 10, i)

            def stream(s0, source, index0, n):
                with sp.Fori(0, n // 4) as m:
                    for j in range(4):
                        load(m * 4 + (s0 + j), source, m * 4 + (index0 + j), (s0 + j) % RING)
                for j in range(n // 4 * 4, n):
                    load(s0 + j, source, index0 + j, (s0 + j) % RING)

            stream(S_UP[0] + 35, io["w_up"], 35, 29)
            stream(S_DN[0], io["w_down"], 0, 32)
            stream(S_UP[1], io["w_up"], 64, 64)
            stream(S_DN[1], io["w_down"], 32, 32)
            stream(S_UP[2], io["w_up"], 128, 40)
            for j in range(8):
                load(S_UP[2] + 40 + j, io["w_up_tail"], j, j % RING, SLAB // 2)
            for g in range(4):
                for j in range(6):
                    s = S_DN[2] + 6 * g + j
                    if j < 5:
                        load(s, io["w_down"], 64 + 5 * g + j, s % RING)
                    else:
                        load(s, io["w_down_tail"], g, s % RING, SLAB // 2)

        @block.scalar
        def _(act):
            def eps_col(i):
                return small[:, 140 + i:141 + i]

            def hi(s, n4, slot, cols=SLAB):
                act.wait_ge(raw_in[slot], n4 * 16 + 16)
                if not isinstance(s, int) or s >= RING:
                    act.wait_ge(used, s - RING + 1)
                o = slot * SLAB
                nc.scalar.activation(wH[:, o:o + cols], raw[:, o:o + cols], ACT.Copy).then_inc(hi_done, 1)

            def hi_ahead(s0, n0, i, end=None, cols=SLAB):
                j = i + AHEAD
                hi(s0 + j, n0 + j // RING, j % RING, cols)

            def ada_copy(unit, rows_turned=0):
                act.wait_ge(ada_used, unit * ADA_STEPS + ADA_STEPS)
                if not isinstance(unit, int) or unit > 0:
                    act.wait_ge(bank_full[7], unit + rows_turned)
                nc.scalar.activation(adaS[:, :], ps[:, 6, 0:256], ACT.Copy).then_inc(adaS_ready, 1)

            def h_hi(kg):
                act.wait_ge(h32_ready, kg + 1)
                nc.scalar.activation(tiles(hH, kg * 4, 4), tiles(H32, 0, 4), ACT.Copy).then_inc(hH_ready, 1)

            act.dma_start(cT[:, :], io["cT"][:, :]).then_inc(c_in, 16)
            act.dma_start(xT[:, :], io["xT"][:, :]).then_inc(x_in, 16)
            act.wait_ge(c_in, 16)
            nc.scalar.activation(cT[:, :], cT[:, :], ACT.Silu).then_inc(c_silu, 1)
            for s in range(AHEAD):
                hi(s, 0, s)
            ada_copy(0)
            h_hi(0)
            hi_ahead(0, 0, 0)
            with act.Fori(0, 3) as kg:
                for i in range(1, IN_STEPS + 1):
                    hi_ahead(kg * IN_STEPS, kg * 5, i)
                    if i == ADA_STEPS + 1:
                        h_hi(kg + 1)
                    if i == ADA_STEPS - 1:
                        ada_copy(kg + 1)
            for i in range(1, IN_STEPS + 1):
                hi_ahead(3 * IN_STEPS, 15, i)
                if i == ADA_STEPS - 1:
                    ada_copy(4)

            act.wait_ge(proj_ready, 1)
            for k in (32, 24):
                v = proj[:, k * ROWS:(k + 8) * ROWS]
                nc.scalar.activation(v, v, ACT.Gelu_apprx_tanh).then_inc(gelu_ready, 1)
            for hg in range(2):
                for r in range(2):
                    b = filled(act, ("v", r, hg))
                    release(nc.scalar.activation(Vrm[:, r * 1024 + hg * 512:r * 1024 + (hg + 1) * 512], b, ACT.Copy), ("v", r, hg))
            act.wait_ge(var_ready, 3)
            nc.scalar.activation(small[:, 42:45], spread(small[:, 37:38], [2, 3]), ACT.Sqrt, bias=eps_col(0)).then_inc(va_sd, 1)
            ada_copy(5)
            ada_copy(6)
            for h in range(HEADS + 1):
                if h < HEADS:
                    act.wait_ge(logit_ready, h + 1)
                    o = (h % 2) * 384
                    nc.scalar.activation(Pp[:, o:o + P], Lp[:, o:o + P], ACT.Exp, bias=small[:, 50 + 2 * (h % 2):51 + 2 * (h % 2)],
                                         accum_out=small[:, 54 + 2 * (h % 2):55 + 2 * (h % 2)])
                    nc.scalar.activation(Pp[:, o + P:o + 384], Lp[:, o + P:o + 384], ACT.Exp, bias=small[:, 51 + 2 * (h % 2):52 + 2 * (h % 2)],
                                         accum_out=small[:, 55 + 2 * (h % 2):56 + 2 * (h % 2)]).then_inc(exp_ready, 1)
                if h:
                    g = h - 1
                    b = filled(act, ("PT", g))
                    o = (g % 2) * 384
                    release(nc.scalar.activation(PTp[:, o:o + 384], b[:, 0:384], ACT.Copy), ("PT", g))
                    b = filled(act, ("PV", g))
                    release(nc.scalar.activation(tile(proj, g, 0, SEQ), b[:, 0:SEQ], ACT.Copy), ("PV", g))
            ada_copy(7)
            ada_copy(8)
            act.wait_ge(s_logit, 1)
            for hh in range(2):
                e = nc.scalar.activation(Ls[:, hh * ROWS:(hh + 1) * ROWS], Ls[:, hh * ROWS:(hh + 1) * ROWS], ACT.Exp,
                                         bias=small[:, 58 + hh:59 + hh], accum_out=small[:, 60 + hh:61 + hh])
            e.then_inc(s_exp, 1)
            b = filled(act, "s PT")
            release(nc.scalar.activation(PTs[:, :], b, ACT.Copy), "s PT")
            act.wait_ge(gm_ready, 1)
            act.wait_ge(kv_stored, 16)
            nc.scalar.activation(tiles(proj, 16, 8), tiles(proj, 24, 8), ACT.Square).then_inc(sq_ready, 1)
            b = filled(act, "OT")
            v = nc.scalar.activation(tiles(proj, 0, 8, SEQ, ROWS), b[:, 0:256].rearrange("p (h c) -> p h c", h=8), ACT.Copy)
            release(v, "OT")
            ada_copy(9)
            released(act, "OT")
            nc.scalar.activation(tiles(proj, 8, 8), tiles(proj, 0, 8), ACT.Square).then_inc(sq_ready, 1)
            for a, job in enumerate(("sum a", "sum b")):
                b = filled(act, job)
                release(nc.scalar.activation(RR[:, a * ROWS:(a + 1) * ROWS], b[:, 0:ROWS], ACT.Sqrt, scale=1.0 / 1024, bias=eps_col(0)), job)
            for k in range(KT):
                act.wait_ge(m_ready, k // 4 + 1)
                src = 24 + k if k < 8 else k - 8
                nc.scalar.activation(tile(hH, k), tile(proj, src), ACT.Copy, scale=vec[:, V_NA + k:V_NA + k + 1]).then_inc(mH_ready, 1)

            def copy_sum(g, ln):
                act.wait_ge(s4_ready, 4 * ln + g + 1)
                nc.scalar.activation(tiles(xT, 4 * g, 4), tiles(S4, 0, 4), ACT.Copy).then_inc(s4_copied, 1)

            for g in range(4):
                for j in range(8):
                    if g or j:
                        hi_ahead(S_OUT, S_OUT // 4, 8 * g + j)
                    if g and j == 0:
                        copy_sum(g - 1, 0)

            def normalise(ln, scale_at, bias_at):
                copy_sum(3, ln)
                act.wait_ge(ln_var, ln + 1)
                nc.scalar.activation(small[:, 130:133], small[:, 126:129], ACT.Sqrt, bias=eps_col(1)).then_inc(ln_sd, 1)
                b = filled(act, ("ln", ln, 0))
                release(nc.scalar.activation(RN[:, 0:ROWS], b[:, 0:ROWS], ACT.Copy), ("ln", ln, 0))

                def affine(b4):
                    act.wait_ge(xn_ready, 4 * ln + b4 + 1)
                    for k in range(4 * b4, 4 * b4 + 4):
                        y = nc.scalar.activation(tile(xT, k), tile(xT, k), ACT.Identity, scale=vec[:, scale_at + k:scale_at + k + 1],
                                                 bias=vec[:, bias_at + k:bias_at + k + 1])
                    y.then_inc(x1_ready, 1)
                return affine

            hi_ahead(S_UP[0], S_UP[0] // 4, 0)
            affine = normalise(0, V_G1, V_B1)
            affine(0)
            for b4 in range(4):
                if b4 < 3:
                    affine(b4 + 1)
                act.wait_ge(h2_32, b4 + 1)
                nc.scalar.activation(tiles(hH, 4 * b4, 4), tiles(H2, 0, 4), ACT.Copy).then_inc(h2H, 1)

            def up_rows(G, job, it, s_last, td, halves=2):
                banks = [0, 1, 2, 3] if halves == 2 else [0, 2]
                act.wait_ge(conv_ready, G * 2 + 2)
                act.wait_ge(tails_ready, G + 1)
                act.wait_ge(pads_set, 1)
                for n, t in enumerate(banks):
                    if n < len(banks) - 1:
                        act.wait_ge(tile_done, td + (n + 1))
                    else:
                        act.wait_ge(used, s_last + 1)
                    o = t * UW
                    nc.scalar.activation(U[:, o + 2:o + 2 + SEQ], ps[:, t, 0:SEQ], ACT.Copy)
                    release(nc.scalar.activation(spread(U[:, o + SEQ + 4:o + SEQ + 5], [TOK + 2, NSEQ], [1, TOK]),
                                                 ps[:, t, SEQ:ROWS].rearrange("p (n t) -> p n t", t=TOK), ACT.Copy), (job, t))

            def up_silu(G, gg, halves=2):
                act.wait_ge(conv_ready, G * 2 + 3)
                w = halves * CW
                nc.scalar.activation(SA[:, 0:w], CV[:, 0:w], ACT.Silu).then_inc(silu_ready, 1)
                act.wait_ge(ff32_ready, G + 1)
                nc.scalar.activation(tiles(ffH, gg * 2, halves), tiles(Ff, 0, halves), ACT.Copy).then_inc(ffH_ready, 1)

            for ph in range(3):
                s0, td, G0 = S_UP[ph], TD_UP[ph], GROUPS_BEFORE[ph]
                if ph == 0:
                    with act.Fori(0, 2) as u:
                        for i in range(1, 17):
                            half = i // 8 - 1
                            if i == 16:
                                ada_copy(u + 10, rows_turned=4)
                            if i % 8 == 0:
                                up_rows(u * 2 + half, ("up", 0, "ab"[half]), u, u * 16 + (s0 + i - 1), u * 6 + (td + 3 * half))
                            hi_ahead(u * 16 + s0, u * 4 + s0 // 4, i)
                            if i % 8 == 0:
                                up_silu(u * 2 + half, u * 2 + half)
                    s1, count, G1st, job, td = s0 + 32, 4, 4, ("up", 0, "c"), td + 12
                else:
                    s1, count, G1st, job = s0, UP_GROUPS[ph], G0, ("up", ph)
                with act.Fori(0, count) as g:
                    for i in range(1, 9):
                        if i == 8:
                            up_rows(g + G1st, job, g, g * 8 + (s1 + 7), g * 3 + td)
                        hi_ahead(g * 8 + s1, g * 2 + s1 // 4, i)
                        if i == 8:
                            up_silu(g + G1st, g + (G1st - G0))
                if ph == 2:
                    for i in range(1, 9):
                        s = S_UP[2] + 40 + i + AHEAD
                        if i == 8:
                            up_rows(G0 + 5, ("up tail",), 0, S_UP[2] + 47, td + 15, halves=1)
                        hi(s, s // 4, s % 4)
                        if i == 8:
                            up_silu(G0 + 5, 5, halves=1)
                if ph < 2:
                    with act.Fori(0, 4) as g:
                        for i in range(1, 9):
                            hi_ahead(g * 8 + S_DN[ph], g * 2 + S_DN[ph] // 4, i)
                else:
                    for g in range(4):
                        for j in range(6):
                            q = 6 * g + j
                            if 0 < q < 24 - AHEAD:
                                s = S_DN[2] + q + AHEAD
                                hi(s, s // 4, s % 4)
                            if g and j == 0:
                                copy_sum(g - 1, 1)
            affine = normalise(1, V_G2, V_B2)
            for b4 in range(4):
                affine(b4)
                act.wait_ge(x1_ready, 4 + b4 + 1)
                act.dma_start(io["yT"][:, b4 * 4 * ROWS:(b4 + 1) * 4 * ROWS], xT[:, b4 * 4 * ROWS:(b4 + 1) * 4 * ROWS]).then_inc(stored, 16)
            act.wait_ge(stored, 16 * 4)



        @block.vector
        def _(dve):
            steps = Steps(dve, dve_step)
            vec_tt, vec_ts, vec_stt = nc.vector.tensor_tensor, nc.vector.tensor_scalar, nc.vector.scalar_tensor_tensor

            def lo(s, slot):
                dve.wait_ge(hi_done, s + 1)
                o = slot * SLAB
                vec_tt(wL[:, o:o + SLAB], raw[:, o:o + SLAB], wH[:, o:o + SLAB].bitcast(F32), ALU.subtract).then_inc(split_done, 1)

            def mod_finish(job, halves, it=0, gate=False):
                b = filled(dve, job, it)
                for half, base_tile in enumerate(halves):
                    src = spread(b[:, 64 * half:64 * half + 1], [32, 2], [P, 2], [1, MODS])
                    if isinstance(base_tile, int):
                        dst, ba = modT[:, base_tile * MODS:(base_tile + 4) * MODS], vec[:, V_ADA + base_tile:V_ADA + base_tile + 4]
                    else:
                        dst, ba = modT[:, bass.ds(base_tile * MODS, 4 * MODS)], vec[:, bass.ds(base_tile + V_ADA, 4)]
                    ins = vec_tt(spread(dst, [2 * MODS, 2], [MODS, 2], [1, MODS]), src, spread(ba, [2, 2], [1, 2], [0, MODS]), ALU.add)
                release(ins, job)
                released(dve, job, it)
                if gate:
                    for base_tile in halves:
                        if isinstance(base_tile, int):
                            v = modT[:, base_tile * MODS:(base_tile + 4) * MODS]
                        else:
                            v = modT[:, bass.ds(base_tile * MODS, 4 * MODS)]
                        ins = vec_ts(v, v, 1.0 / ALPHA, None, ALU.mult)
                    steps.link(ins)

            def modulate(dst, src, scale_tile, shift_tile, k, done):
                dp, dd = tiles(dst, 0, 4, 0, SEQ), by_seq(tiles(dst, 0, 4, SEQ, ROWS), 4)
                scale, shift = mods(scale_tile, 4), mods(shift_tile, 4)
                vec_tt(dp, tiles(src, k, 4, 0, SEQ), scale[0], ALU.mult)
                steps.link(vec_tt(dd, by_seq(tiles(src, k, 4, SEQ, ROWS), 4), scale[1], ALU.mult))
                vec_tt(dp, dp, shift[0], ALU.add)
                vec_tt(dd, dd, shift[1], ALU.add).then_inc(done, 1)

            def h_lo(kg):
                dve.wait_ge(hH_ready, kg + 1)
                vec_tt(tiles(hL, kg * 4, 4), tiles(H32, 0, 4), tiles(hH, kg * 4, 4).bitcast(F32), ALU.subtract).then_inc(h_ready, 1)

            for bank in range(5):
                dve.sem_inc(bank_free[bank], 1)
            dve.sem_inc(conv_ready, 2)
            nc.vector.memset(ones[:, :], 1.0)
            nc.vector.memset(small[:, :], 1.0)
            steps.link(nc.vector.memset(cw[:, :], 0.0))
            nc.vector.memset(small[:, 140:141], EPS)
            nc.vector.memset(small[:, 141:142], EPS / ALPHA ** 2)
            dve.wait_ge(small_in, 16 * 5)
            for scale_at in (V_ADA + 16, V_ADA + SC2):
                vec_ts(vec[:, scale_at:scale_at + 16], vec[:, scale_at:scale_at + 16], 1.0, None, ALU.add)
            w = wsT[:, :].rearrange("p (g t) -> p g t", g=HEADS)
            vec_tt(w, w, spread(cst[:, C_TRI:C_TRI + P], [0, HEADS], [1, P]), ALU.mult)
            w = bd[:, :].rearrange("p (g t) -> p g t", g=HEADS)
            steps.link(vec_tt(w, w, spread(cst[0:SAMP, C_BD:C_BD + SAMP], [0, HEADS], [1, SAMP]), ALU.mult))
            b = filled(dve, "bias")
            nc.vector.tensor_copy(bvec[:, 0:REL_N], spread(b[0:HEADS, REL_N - 1:REL_N], [-1, REL_N]))
            release(nc.vector.tensor_copy(bvec[:, REL_N:2 * REL_N], b[0:HEADS, 0:REL_N]), "bias")
            for s in range(AHEAD):
                lo(s, s)
            mod_finish(("turn", 0), (0, 16))
            dve.wait_ge(x_in, 16)
            modulate(H32, xT, 16, 0, 0, h32_ready)
            h_lo(0)

            dve.wait_ge(proj_zeroed, 1)

            def w_in_quarter(kg, it, loop):
                for i in range(1, IN_STEPS + 1):
                    lo(kg * IN_STEPS + (i + AHEAD), (i + AHEAD) % RING)
                    if i == ADA_STEPS + 2 and loop:
                        h_lo(kg + 1)
                    if i % 2:
                        g = i // 2
                        for t in range(4):
                            if t < 3:
                                dve.wait_ge(tile_done, kg * 30 + (TD_IN + 3 * g + t + 1))
                            else:
                                dve.wait_ge(used, kg * IN_STEPS + (i + 1))
                            k = 4 * g + t
                            release(vec_tt(tile(proj, k), ps[:, k % 5, 0:ROWS], tile(proj, k), ALU.add), ("in", loop, k))
                    if i == ADA_STEPS:
                        if loop:
                            mod_finish(("turn in", loop), (kg * 4 + 4, kg * 4 + 20), it)
                            modulate(H32, xT, kg * 4 + 20, kg * 4 + 4, kg * 4 + 4, h32_ready)
                        else:
                            mod_finish(("turn in", loop), (G1, G1 + 4), it, gate=True)

            lo(AHEAD, AHEAD)
            with dve.Fori(0, 3) as kg:
                steps.enter(kg, 1)
                w_in_quarter(kg, kg, True)
                steps.leave(3)
            w_in_quarter(3, 0, False)
            nc.vector.memset(small[:, 159:160], 0.0).then_inc(proj_ready, 1)

            dve.wait_ge(bvec_stored, 16)
            for hg in range(2):
                b = filled(dve, ("v", 2, hg))
                release(nc.vector.tensor_copy(Vn[:, hg * 512:(hg + 1) * 512], b[0:SAMP, :]), ("v", 2, hg))
            for r in range(3):
                n = P if r < 2 else SAMP
                for hg in range(2):
                    b = filled(dve, ("va", r, hg))
                    ins = nc.vector.bn_stats(small[0:n, 12 * r + 6 * hg:12 * r + 6 * hg + 6], b[0:n, :])
                steps.link(ins)
                nc.vector.bn_aggr(small[0:n, 36 + 2 * r:38 + 2 * r], small[0:n, 12 * r:12 * r + 12]).then_inc(var_ready, 1)
            dve.wait_ge(va_sd, 1)
            steps.link(nc.vector.reciprocal(small[:, 42:45], small[:, 42:45]))
            dve.wait_ge(sgu_in, 16 * 3)
            for r in range(3):
                n = P if r < 2 else SAMP
                dst = VA[:, r * 1024:(r + 1) * 1024] if r < 2 else VAs[:, :]
                for hg in range(2):
                    b = filled(dve, ("va", r, hg))
                    ins = vec_ts(dst[:, hg * 512:(hg + 1) * 512], b[0:n, :], small[0:n, 36 + 2 * r:37 + 2 * r],
                                 small[0:n, 42 + r:43 + r], ALU.subtract, ALU.mult)
                    release(ins, ("va", r, hg))
                released(dve, ("va", r, 1))
                steps.link(vec_tt(dst, dst, SG[0:n, :], ALU.mult))
                vec_tt(dst, dst, SH[0:n, :], ALU.add).then_inc(va_ready, 1)
            mod_finish(("turn", 5), (G1 + 8, G1 + 12), gate=True)

            dve.wait_ge(gelu_ready, 2)
            for c in range(2):
                for gg in range(2):
                    b = filled(dve, ("gate", c, gg))
                    release(vec_tt(Tm[:, gg * 512:(gg + 1) * 512], b, BS[:, gg * 512:(gg + 1) * 512], ALU.add), ("gate", c, gg))
                for gg in range(2):
                    released(dve, ("gate", c, gg))
                    u = tiles(proj, 24 + 4 * gg, 4, c * P, (c + 1) * P)
                    ins = vec_tt(u, u, Tm[:, gg * 512:(gg + 1) * 512].rearrange("p (g t) -> p g t", g=4), ALU.mult)
                steps.link(ins)
            b = filled(dve, "gate decode")
            release(vec_tt(spread(Tm[:, 0:1], [SAMP, HEADS], [TOK, NSEQ], [1, TOK]), spread(b[:, 0:1], [SAMP, HEADS], [TOK, NSEQ], [1, TOK]),
                           spread(BS[:, 0:1], [P, HEADS], [0, NSEQ], [1, TOK]), ALU.add), "gate decode")
            released(dve, "gate decode")
            u = tiles(proj, 24, 8, SEQ, ROWS)
            vec_tt(u, u, Tm[:, 0:256].rearrange("p (g t) -> p g t", g=HEADS), ALU.mult).then_inc(gm_ready, 1)
            mod_finish(("turn", 6), (SH2, SH2 + 4))

            dve.wait_ge(table_in, TABLES * 16)
            for h in range(HEADS + 1):
                if h < HEADS:
                    o, m = (h % 2) * 384, 50 + 2 * (h % 2)
                    if h >= 2:
                        dve.wait_ge(exp_ready, h - 1)
                    b = filled(dve, ("S", h))
                    vec_stt(Lp[:, o:o + P], b[:, 0:P], SCALE, spread(TB[:, h * 256 + P - 1:h * 256 + P], [-1, P]), ALU.mult, ALU.add)
                    release(vec_stt(Lp[:, o + P:o + 384], b[:, P:384], SCALE, spread(TB[:, h * 256 + 255:h * 256 + 256], [-1, 256]), ALU.mult, ALU.add), ("S", h))
                    released(dve, ("S", h))
                    nc.vector.tensor_reduce(small[:, m:m + 1], Lp[:, o:o + P], AX.X, ALU.max, negate=True)
                    nc.vector.tensor_reduce(small[:, m + 1:m + 2], Lp[:, o + P:o + 384], AX.X, ALU.max, negate=True).then_inc(logit_ready, 1)
                if h:
                    o, m = ((h - 1) % 2) * 384, 54 + 2 * ((h - 1) % 2)
                    dve.wait_ge(exp_ready, h)
                    steps.link(nc.vector.reciprocal(small[:, m:m + 2], small[:, m:m + 2]))
                    vec_ts(Pp[:, o:o + P], Pp[:, o:o + P], small[:, m:m + 1], None, ALU.mult)
                    vec_ts(Pp[:, o + P:o + 384], Pp[:, o + P:o + 384], small[:, m + 1:m + 2], None, ALU.mult).then_inc(prob_ready, 1)
            mod_finish(("turn", 7), (SH2 + 8, SH2 + 12))

            sbn = spread(SBi[:, PAST:PAST + 1], [ROWS, 2], [TOK, NSEQ], [1, TOK])
            steps.link(vec_tt(sbn, spread(E4[:, 0:1], [TOK, 2], [0, NSEQ], [1, TOK]),
                              spread(cst[:, C_MP:C_MP + 1], [0, 2], [TOK, NSEQ], [1, TOK]), ALU.mult))
            steps.link(vec_tt(sbn, sbn, spread(cst[:, C_MN:C_MN + 1], [0, 2], [TOK, NSEQ], [1, TOK]), ALU.add))
            for n in range(NSEQ):
                if n >= 2:
                    dve.wait_ge(kv_used, n - 1)
                q = Qm[:, (n % 2) * 256:(n % 2 + 1) * 256].rearrange("p (h c) -> p h c", h=HEADS)
                vec_tt(q, tiles(proj, 0, 8, SEQ, ROWS), spread(cst[:, C_M32 + n * SAMP:C_M32 + n * SAMP + 1], [0, HEADS], [1, SAMP]),
                       ALU.mult).then_inc(qm_ready, 1)
            b = filled(dve, "S new")
            release(vec_stt(spread(Ls[:, PAST:PAST + 1], [ROWS, 2], [1, SAMP]), spread(b[:, 0:1], [SAMP, 2], [1, SAMP]), SCALE,
                            spread(SBi[:, PAST:PAST + 1], [ROWS, 2], [1, SAMP]), ALU.mult, ALU.add), "S new")
            dve.wait_ge(kv_used, NSEQ)
            for hh in range(2):
                release(vec_stt(Ls[:, hh * ROWS:hh * ROWS + PAST], ps[:, hh, 0:PAST], SCALE, SBi[:, hh * ROWS:hh * ROWS + PAST],
                                ALU.mult, ALU.add), f"S past {hh}")
            released(dve, "S past 1")
            nc.vector.tensor_reduce(small[:, 58:60], Ls[:, :].rearrange("p (a c) -> p a c", a=2), AX.X, ALU.max, negate=True).then_inc(s_logit, 1)
            mod_finish(("turn", 8), (SC2, SC2 + 4))
            dve.wait_ge(s_exp, 1)
            steps.link(nc.vector.reciprocal(small[:, 60:62], small[:, 60:62]))
            for hh in range(2):
                ins = vec_ts(Ls[:, hh * ROWS:(hh + 1) * ROWS], Ls[:, hh * ROWS:(hh + 1) * ROWS], small[:, 60 + hh:61 + hh], None, ALU.mult)
            ins.then_inc(s_prob, 1)
            b = filled(dve, "s PN")
            release(nc.vector.tensor_copy(PN[:, :], b[0:SAMP, 0:256]), "s PN")
            released(dve, "s PT")
            for n in range(NSEQ):
                if n >= 2:
                    dve.wait_ge(kv_used, NSEQ + n - 1)
                vec_tt(PTm[:, (n % 2) * 512:(n % 2 + 1) * 512].rearrange("p (a c) -> p a c", a=16),
                       PTs[:, :].rearrange("p (a c) -> p a c", a=16),
                       spread(cst[:, C_M32 + n * SAMP:C_M32 + n * SAMP + 1], [0, 16], [1, SAMP]), ALU.mult).then_inc(ptm_ready, 1)
            for hh in range(2):
                b = filled(dve, f"O {hh}")
                release(nc.vector.tensor_copy(OS[:, hh * P:(hh + 1) * P], b[:, 0:P]), f"O {hh}")
            mod_finish(("turn", 9), (SC2 + 8, SC2 + 12))

            for a, job in enumerate(("sum a", "sum b")):
                released(dve, job)
                rr = RR[:, a * ROWS:(a + 1) * ROWS]
                steps.link(nc.vector.reciprocal(rr, rr))
                for half in range(2):
                    m = tiles(proj, (24, 0)[a] + 4 * half, 4)
                    vec_tt(m, m, spread(rr, [0, 4], [1, ROWS]), ALU.mult).then_inc(m_ready, 1)
                for k in range(8 * a, 8 * a + 8):
                    dve.wait_ge(mH_ready, k + 1)
                    vec_stt(tile(hL, k), tile(proj, 24 + k if k < 8 else k - 8), vec[:, V_NA + k:V_NA + k + 1],
                            tile(hH, k).bitcast(F32), ALU.mult, ALU.subtract).then_inc(m_split, 1)

            def residual(g, ln, job, gate_tile, td, s_last):
                for t in range(3):
                    dve.wait_ge(tile_done, td + t + 1)
                dve.wait_ge(used, s_last + 1)
                if ln or g:
                    dve.wait_ge(s4_copied, 4 * ln + g)
                samp = by_seq(tiles(S4, 0, 4, SEQ, ROWS), 4)
                gates = mods(gate_tile + 4 * g, 4)[1]
                steps.link(vec_tt(samp, ps[:, 0:4, SEQ:ROWS].rearrange("p k (n t) -> p k n t", t=TOK), gates, ALU.mult))
                for t in range(4):
                    c = (gate_tile + 4 * g + t) * MODS
                    release(vec_stt(tile(S4, t, 0, SEQ), ps[:, t, 0:SEQ], modT[:, c:c + 1], tile(xT, 4 * g + t, 0, SEQ), ALU.mult, ALU.add),
                            job(t))
                vec_tt(tiles(S4, 0, 4, SEQ, ROWS), tiles(S4, 0, 4, SEQ, ROWS), tiles(xT, 4 * g, 4, SEQ, ROWS), ALU.add).then_inc(s4_ready, 1)

            def row_statistics(g, ln):
                for r in range(3):
                    n, job = P if r < 2 else SAMP, ("rows", ln, g, r)
                    b = filled(dve, job)
                    release(nc.vector.bn_stats(small[0:n, 50 + 24 * r + 6 * g:56 + 24 * r + 6 * g], b[0:n, :]), job)

            def normalise(ln):
                row_statistics(3, ln)
                released(dve, ("rows", ln, 3, 2))
                for r in range(3):
                    n = P if r < 2 else SAMP
                    ins = nc.vector.bn_aggr(small[0:n, 134 + 2 * r:136 + 2 * r], small[0:n, 50 + 24 * r:74 + 24 * r])
                steps.link(ins)
                nc.vector.tensor_copy(small[:, 126:129], spread(small[:, 135:136], [2, 3])).then_inc(ln_var, 1)
                dve.wait_ge(ln_sd, ln + 1)
                steps.link(nc.vector.reciprocal(small[:, 142:145], small[:, 130:133]))
                steps.link(vec_stt(small[:, 145:148], spread(small[:, 134:135], [2, 3]), -1.0, small[:, 142:145], ALU.mult, ALU.mult))
                for r in range(3):
                    n = P if r < 2 else SAMP
                    for j in range(2):
                        ins = vec_ts(DG[0:n, (2 * r + j) * P:(2 * r + j) * P + n], ident[0:n, 0:n],
                                     small[0:n, 142 + 3 * j + r:143 + 3 * j + r], None, ALU.mult)
                ins.then_inc(diag_ready, 1)
                b = filled(dve, ("ln", ln, 1))
                dve.wait_ge(s4_copied, 4 * ln + 4)
                release(nc.vector.tensor_copy(RN[:, ROWS:2 * ROWS], b[:, 0:ROWS]), ("ln", ln, 1))
                released(dve, ("ln", ln, 0))
                released(dve, ("ln", ln, 1))

            def centre(b4, ln):
                x = tiles(xT, 4 * b4, 4)
                steps.link(vec_tt(x, x, spread(RN[:, 0:1], [0, 4], [1, ROWS]), ALU.mult))
                vec_tt(x, x, spread(RN[:, ROWS:ROWS + 1], [0, 4], [1, ROWS]), ALU.add).then_inc(xn_ready, 1)

            dve.wait_ge(va_stored, 16)
            for g in range(4):
                for j in range(8):
                    if g or j:
                        lo(S_OUT + 8 * g + j + AHEAD, (j + AHEAD) % RING)
                    if g and j == 3:
                        row_statistics(g - 1, 0)
                residual(g, 0, lambda t: ("out", g, t), G1, TD_OUT + 3 * g, S_OUT + 8 * g + 7)
            lo(S_UP[0] + AHEAD, AHEAD)
            normalise(0)
            centre(0, 0)
            for b4 in range(4):
                if b4 < 3:
                    centre(b4 + 1, 0)
                dve.wait_ge(x1_ready, b4 + 1)
                if b4:
                    dve.wait_ge(h2_ready, b4)
                modulate(H2, xT, SC2 + 4 * b4, SH2 + 4 * b4, 4 * b4, h2_32)
                dve.wait_ge(h2H, b4 + 1)
                vec_tt(tiles(hL, 4 * b4, 4), tiles(H2, 0, 4), tiles(hH, 4 * b4, 4).bitcast(F32), ALU.subtract).then_inc(h2_ready, 1)

            def convolve(G, job, it, halves):
                dve.wait_ge(past_ready, G + 1)
                for pair in range(2):
                    both = [2 * pair, 2 * pair + 1][:halves]
                    for t in both:
                        released(dve, (job, t), it)
                    cv, u = lambda t: CV[:, t * CW:(t + 1) * CW], lambda t, d: U[:, t * UW + d:t * UW + d + CW]
                    for t in both:
                        ins = vec_ts(cv(t), u(t, 0), cw[:, 4 * t:4 * t + 1], cw[:, 4 * t + 3:4 * t + 4], ALU.mult, ALU.add)
                    steps.link(ins)
                    for t in both:
                        ins = vec_stt(cv(t), u(t, 1), cw[:, 4 * t + 1:4 * t + 2], cv(t), ALU.mult, ALU.add)
                    steps.link(ins)
                    for t in both:
                        ins = vec_stt(cv(t), u(t, 2), cw[:, 4 * t + 2:4 * t + 3], cv(t), ALU.mult, ALU.add)
                    ins.then_inc(conv_ready, 1)

            def gated(G, gg, halves):
                dve.wait_ge(silu_ready, G + 1)
                dve.wait_ge(conv_ready, G * 2 + 4)
                a, v = SA[:, 0:halves * CW].rearrange("p (k c) -> p k c", k=halves), CV[:, 2 * CW:(2 + halves) * CW].rearrange("p (k c) -> p k c", k=halves)
                rows = lambda x: spread(x[:, :, SEQ + 2:SEQ + 3], [CW, halves], [TOK + 2, NSEQ], [1, TOK])
                vec_tt(tiles(Ff, 0, halves, 0, SEQ), a[:, :, 0:SEQ], v[:, :, 0:SEQ], ALU.mult)
                vec_tt(by_seq(tiles(Ff, 0, halves, SEQ, ROWS), halves), rows(a), rows(v), ALU.mult).then_inc(ff32_ready, 1)
                dve.wait_ge(ffH_ready, G + 1)
                vec_tt(tiles(ffL, gg * 2, halves), tiles(Ff, 0, halves), tiles(ffH, gg * 2, halves).bitcast(F32),
                       ALU.subtract).then_inc(ff_ready, 1)

            def accumulate(g, ph, td, s_last):
                for t in range(3):
                    dve.wait_ge(tile_done, td + (t + 1))
                dve.wait_ge(used, s_last + 1)
                nc.vector.tensor_copy(small[:, 148:152], spread(modT[:, bass.ds(g * (4 * MODS) + G2 * MODS, 1)], [MODS, 4]))
                gates = spread(modT[:, bass.ds(g * (4 * MODS) + (G2 * MODS + 1), 1)], [MODS, 4], [1, NSEQ], [0, TOK])
                S4d = tiles(S4, 0, 4, SEQ, ROWS)
                steps.link(vec_tt(by_seq(S4d, 4), ps[:, 0:4, SEQ:ROWS].rearrange("p k (n t) -> p k n t", t=TOK), gates, ALU.mult))
                for t in range(4):
                    x = xT[:, bass.ds(g * (4 * ROWS) + t * ROWS, SEQ)]
                    release(vec_stt(x, ps[:, t, 0:SEQ], small[:, 148 + t:149 + t], x, ALU.mult, ALU.add), ("down", ph, t))
                x = tiles(xT, g * 4, 4, SEQ, ROWS)
                vec_tt(x, x, S4d, ALU.add)

            for ph in range(3):
                s0, G0 = S_UP[ph], GROUPS_BEFORE[ph]
                if ph == 0:
                    with dve.Fori(0, 2) as u:
                        steps.enter(u, 9)
                        for i in range(1, 17):
                            if i % 8 == 0:
                                convolve(u * 2 + i // 8 - 1, ("up", 0, "ab"[i // 8 - 1]), u, 2)
                            lo(u * 16 + (s0 + i + AHEAD), (i + AHEAD) % RING)
                            if i % 8 == 0:
                                gated(u * 2 + i // 8 - 1, u * 2 + i // 8 - 1, 2)
                        mod_finish(("turn up",), (u * 8 + G2, u * 8 + (G2 + 4)), u, gate=True)
                        steps.leave(2)
                    loops = [(4, s0 + 32, 4, ("up", 0, "c"))]
                else:
                    loops = [(UP_GROUPS[ph], s0, G0, ("up", ph))]
                for count, s1, G1st, job in loops:
                    with dve.Fori(0, count) as g:
                        steps.enter(g, 4)
                        for i in range(1, 9):
                            if i == 8:
                                convolve(g + G1st, job, g, 2)
                            lo(g * 8 + (s1 + i + AHEAD), (i + AHEAD) % RING)
                            if i == 8:
                                gated(g + G1st, g + (G1st - G0), 2)
                        steps.leave(count)
                if ph == 2:
                    for i in range(1, 9):
                        s = S_UP[2] + 40 + i + AHEAD
                        if i == 8:
                            convolve(G0 + 5, ("up tail",), 0, 1)
                        lo(s, s % RING)
                        if i == 8:
                            gated(G0 + 5, 5, 1)
                if ph < 2:
                    with dve.Fori(0, 4) as g:
                        steps.enter(g, 1)
                        for i in range(1, 9):
                            if i == 8:
                                accumulate(g, ph, g * 3 + TD_DN[ph], g * 8 + (S_DN[ph] + 7))
                            lo(g * 8 + (S_DN[ph] + i + AHEAD), (i + AHEAD) % RING)
                        steps.leave(4)
                else:
                    for g in range(4):
                        for j in range(6):
                            q = 6 * g + j
                            if 0 < q < 24 - AHEAD:
                                lo(S_DN[2] + q + AHEAD, (S_DN[2] + q + AHEAD) % RING)
                            if g and j == 3:
                                row_statistics(g - 1, 1)
                        residual(g, 1, lambda t: ("down", 2, g, t), G2, TD_DN[2] + 3 * g, S_DN[2] + 6 * g + 5)
            normalise(1)
            for b4 in range(4):
                centre(b4, 1)

        @block.gpsimd
        def _(pool):
            copy = nc.gpsimd.tensor_copy
            pool.sem_inc(tails_ready, 1)
            pool.dma_start(cst[:, :], io["cst"][:, :]).then_inc(small_in, 16)
            pool.dma_start(vec[:, :], io["vec"][:, :]).then_inc(small_in, 16)
            pool.dma_start(hot[:, :], io["hot"][:, :]).then_inc(bias_in, 16)
            pool.dma_start(rbias[:, :], io["rbias"][:, :]).then_inc(bias_in, 16)
            pool.dma_start(wsT[:, :], io["wsT"][:, :]).then_inc(small_in, 16)
            pool.dma_start(bd[:, :], io["bd"][:, :]).then_inc(small_in, 16)
            pool.dma_start(past[:, :], io["past"][:, :]).then_inc(small_in, 16)
            pool.dma_start(pages[:, :], io["pages"][:, :]).then_inc(pages_in, 16)
            nc.gpsimd.memset(proj[:, :], 0.0).then_inc(proj_zeroed, 1)
            released(pool, "bias")
            pool.dma_start(bias_rows[:, :].rearrange("(a h) c -> h a c", a=2), bvec[:, :].rearrange("h (a c) -> h a c", a=2)).then_inc(bvec_stored, 16)

            pool.wait_ge(proj_ready, 1)
            for at, name in ((SG, "sgu_g"), (SH, "sgu_b"), (BS, "b_s")):
                pool.dma_start(at[:, :], bass.AP(io[name].tensor, 0, [[0, P], [1, 1024]])).then_inc(sgu_in, 16)
            pool.wait_ge(pages_in, 16)

            def load_kv(idx):
                n, name = idx % NSEQ, "keys" if idx < NSEQ else "values"
                if idx >= 2:
                    pool.wait_ge(kv_used, idx - 1)
                for pg in range(PAGES):
                    page = pool.value_load(pages[0:1, n * PAGES + pg:n * PAGES + pg + 1], min_val=0, max_val=n_phys - 1)
                    o = (idx % 2) * 2048 + pg * 1024
                    pool.dma_start(KV[:, o:o + 1024], io[name][bass.ds(page, 1), :, :].rearrange("a p c -> (a p) c")).then_inc(kv_in[idx % 2], 16)

            load_kv(0)
            load_kv(1)
            pool.dma_start(io["kvT"][:, :], proj[:, 8 * ROWS:24 * ROWS]).then_inc(kv_stored, 16)
            pool.wait_ge(va_ready, 3)
            pool.dma_start(io["va"][:, :], VAs[:, :]).then_inc(va_stored, 16)
            pool.wait_ge(bvec_stored, 16)
            pool.wait_ge(gm_ready, 1)
            rows = bias_rows.tensor
            pool.dma_start(TB[:, :].rearrange("p (h c) -> p h c", h=HEADS),
                           bass.AP(rows, 0, [[1, P], [REL_N, HEADS], [1, 256]])).then_inc(table_in, 16)
            for hh in range(2):
                for t in range(TOK):
                    pool.dma_start(SBi[t:P:TOK, hh * ROWS:hh * ROWS + PAST],
                                   bass.AP(rows, HEADS * REL_N + 4 * hh * REL_N + TOK - 1 - t, [[REL_N, 4], [0, NSEQ], [1, PAST]])).then_inc(table_in, 16)
                    pool.dma_start(E4[t:P:TOK, hh * TOK:(hh + 1) * TOK],
                                   bass.AP(rows, HEADS * REL_N + 4 * hh * REL_N + REL_MAX - t, [[REL_N, 4], [0, NSEQ], [1, TOK]])).then_inc(table_in, 16)
            for idx in range(2, 2 * NSEQ):
                load_kv(idx)

            pool.wait_ge(m_ready, 1)
            nc.gpsimd.memset(spread(U[:, 0:1], [UW, 4], [1, 2]), 0.0).then_inc(pads_set, 1)

            def flat(t, k, step, n):
                return t[:, k * step:(k + n) * step] if isinstance(k, int) else t[:, bass.ds(k * step, n * step)]

            def group(G, job, it, halves=2):
                pool.wait_ge(conv_ready, G * 2 + 2)
                for pair, first in ((0, G * 2), (1, G * 2 + FT)):
                    copy(spread(U[:, 2 * pair * UW + SEQ + 2:2 * pair * UW + SEQ + 3], [UW, halves], [TOK + 2, NSEQ], [1, 2]),
                         spread(flat(past, first, 16, halves), [16, halves], [2, NSEQ], [1, 2]))
                    ins = copy(cw[:, 8 * pair:8 * pair + 4 * halves], flat(taps, first, 4, halves))
                ins.then_inc(past_ready, 1)
                for pair, first in ((0, G * 2), (1, G * 2 + FT)):
                    for t in range(2 * pair, 2 * pair + halves):
                        released(pool, (job, t), it)
                    e = flat(E, first, 18, halves)
                    o = 2 * pair * UW
                    copy(spread(e, [18, halves], [1, 2]), spread(U[:, o + SEQ:o + SEQ + 1], [UW, halves], [1, 2]))
                    ins = copy(spread(e.rearrange("p (k c) -> p k c", k=halves)[:, :, 2:18], [18, halves], [2, NSEQ], [1, 2]),
                               spread(U[:, o + SEQ + 6:o + SEQ + 7], [UW, halves], [TOK + 2, NSEQ], [1, 2]))
                ins.then_inc(tails_ready, 1)

            taps = vec[:, V_CONV:V_ALL]
            with pool.Fori(0, 2) as u:
                group(u * 2, ("up", 0, "a"), u)
                group(u * 2 + 1, ("up", 0, "b"), u)
            with pool.Fori(0, 4) as g:
                group(g + 4, ("up", 0, "c"), g)
            for ph in (1, 2):
                with pool.Fori(0, UP_GROUPS[ph]) as g:
                    group(g + GROUPS_BEFORE[ph], ("up", ph), g)
            group(GROUPS_BEFORE[2] + 5, ("up tail",), 0, 1)
            pool.wait_ge(tails_ready, GROUPS_BEFORE[2] + 7)
            pool.dma_start(io["tails"][:, :], E[:, :]).then_inc(tails_stored, 16)
            pool.wait_ge(tails_stored, 16)
            pool.wait_ge(kv_stored, 16)
            pool.wait_ge(va_stored, 16)


def kernel(**inputs):
    from concourse import bacc
    from concourse.bass_utils import run_bass_kernel_spmd

    a = {k: np.asarray(v) for k, v in inputs.items()}
    f = np.ascontiguousarray

    def rows_t(p, s):
        x = np.concatenate([p.reshape(SEQ, -1), s.reshape(SAMP, -1)], 0)
        return f(x.T.reshape(-1, P, ROWS).transpose(1, 0, 2).reshape(P, -1))

    D_IN = a["w_in"].shape[2] // P
    w_in = a["w_in"][0].reshape(KT, P, D_IN, P)
    w_in_s = f(np.stack([w_in[4 * kg + 2 * half:4 * kg + 2 * half + 2, :, 4 * g:4 * g + 4].transpose(1, 0, 2, 3).reshape(P, -1)
                         for kg in range(4) for g in range(IN_GROUPS) for half in range(2)]))
    w_out = a["w_out"][0]
    w_up = a["w_up"][0]
    w_down = a["w_down"][0]
    tile_of = lambda k: slice(k * P, (k + 1) * P)

    def slab(w, ks, ns):
        return np.stack([w[tile_of(k)][:, np.concatenate([np.arange(n * P, (n + 1) * P) for n in ns])] for k in ks], 1).reshape(P, -1)

    w_out_s = f(np.stack([slab(w_out, (2 * j, 2 * j + 1), range(4 * g, 4 * g + 4)) for g in range(4) for j in range(8)]))
    up_tiles = [[16 * ph + 2 * gg, 16 * ph + 2 * gg + 1, FT + 16 * ph + 2 * gg, FT + 16 * ph + 2 * gg + 1]
                for ph in range(3) for gg in range(UP_GROUPS[ph])]
    w_up_s = f(np.stack([slab(w_up, (2 * j, 2 * j + 1), ns) for ns in up_tiles for j in range(8)]))
    w_up_tail = f(np.stack([slab(w_up, (2 * j, 2 * j + 1), (FT - 1, 2 * FT - 1)) for j in range(8)]))
    down = [(2 * j, g) for g in range(4) for j in range(8)] + [(16 + 2 * j, g) for g in range(4) for j in range(8)] + \
           [(32 + 2 * j, g) for g in range(4) for j in range(5)]
    w_down_s = f(np.stack([slab(w_down, (k, k + 1), range(4 * g, 4 * g + 4)) for k, g in down]))
    w_down_tail = f(np.stack([slab(w_down, (FT - 1,), range(4 * g, 4 * g + 4)) for g in range(4)]))
    w_ada = a["w_ada"][0]
    units = [[slice(512 * u, 512 * u + 512), slice(D + 512 * u, D + 512 * u + 512)] for u in range(4)] + \
            [[slice(2 * D + 1024 * w, 2 * D + 1024 * w + 1024)] for w in range(8)]
    w_ada_s = f(np.concatenate([np.concatenate([w_ada[:, c] for c in cols], 1).reshape(KT, P, 1024) for cols in units]))

    c = np.zeros((32, D), np.float32)
    c[:1], c[1:MODS] = a["c_prompt"], a["c_sample"]
    col = lambda v: v.reshape(-1, P).T
    taps = np.concatenate([a["w_conv"][0], a["b_conv"]], 0).reshape(4, 2 * FT, P).transpose(2, 1, 0).reshape(P, -1)
    vec = np.concatenate([col(a["b_ada"]), col(a["ln1_g"]), col(a["ln1_b"]), col(a["norm_a_g"]), col(a["norm_b_g"]),
                          col(a["ln2_g"]), col(a["ln2_b"]), taps], 1)
    ws = a["w_s"][0]
    bd = np.zeros((NSEQ, TOK, HEADS, NSEQ, TOK), np.float32)
    for n in range(NSEQ):
        bd[n, :, :, n, :] = ws[:, :TOK, :TOK].transpose(2, 0, 1)
    cst, hot = shape_constants()
    n_phys = a["cache_k"].shape[1]
    arrays = {
        "xT": rows_t(a["x_prompt"], a["x_sample"]),
        "cT": f(c.T.reshape(KT, P, 32).transpose(1, 0, 2).reshape(P, -1)),
        "w_ada": w_ada_s, "w_in": w_in_s, "w_out": w_out_s, "w_up": w_up_s, "w_up_tail": w_up_tail,
        "w_down": w_down_s, "w_down_tail": w_down_tail,
        "vec": f(vec), "cst": cst, "hot": hot,
        "rbias": f(np.concatenate([a["rel_bias"], np.full((1, HEADS), NEG, np.float32)], 0)),
        "wsT": f(ws.transpose(2, 0, 1).reshape(P, -1)), "bd": f(bd.reshape(SAMP, -1)),
        "sgu_g": f(a["ln_sgu_g"]), "sgu_b": f(a["ln_sgu_b"]), "b_s": f(a["b_s"].reshape(1, -1)),
        "past": f(a["state_ffn_conv"][0].reshape(NSEQ, 2, 2 * FT, P).transpose(3, 2, 0, 1).reshape(P, -1)),
        "pages": f(a["page_table"].reshape(1, -1)),
        "keys": f(a["cache_k"][0].transpose(0, 3, 2, 1).reshape(n_phys, P, -1)),
        "values": f(a["cache_v"][0].reshape(n_phys, P, -1)),
    }
    outs = {"yT": [P, KT * ROWS], "kvT": [P, 16 * ROWS], "va": [SAMP, 1024], "tails": [P, 2 * FT * 18]}
    nc = bacc.Bacc("TRN2", target_bir_lowering=False, num_devices=1)
    io = {k: nc.dram_tensor(k, v.shape, mybir.dt.from_np(v.dtype), kind="ExternalInput").ap() for k, v in arrays.items()}
    io.update({k: nc.dram_tensor(k, s, F32, kind="ExternalOutput").ap() for k, s in outs.items()})
    decoder_layer_program(nc, io, n_phys)
    r = run_bass_kernel_spmd(nc, [arrays], core_ids=[0]).results[0]

    def rows_of(t, n):
        x = t.reshape(P, n, ROWS).transpose(2, 1, 0).reshape(ROWS, n * P)
        return f(x[:SEQ]), f(x[SEQ:])

    y_p, y_s = rows_of(np.asarray(r["yT"]), KT)
    kv_p, kv_s = rows_of(np.asarray(r["kvT"]), 16)
    tails = np.asarray(r["tails"]).reshape(P, 2 * FT, 18)
    conv_p = f(tails[:, :, :2].transpose(2, 1, 0)).reshape(1, 1, 2, 2 * FF)
    conv_s = f(tails[:, :, 2:].reshape(P, 2 * FT, NSEQ, 2).transpose(2, 3, 1, 0)).reshape(1, NSEQ, 2, 2 * FF)
    half = HEADS * P
    return (y_p.reshape(1, SEQ, D), y_s.reshape(NSEQ, TOK, D),
            f(kv_p[:, :half]).reshape(1, 1, SEQ, HEADS, P), f(kv_p[:, half:]).reshape(1, 1, SEQ, HEADS, P), conv_p,
            f(kv_s[:, :half]).reshape(1, NSEQ, TOK, HEADS, P), f(kv_s[:, half:]).reshape(1, NSEQ, TOK, HEADS, P),
            np.asarray(r["va"]).reshape(1, NSEQ, TOK, 1024), conv_s)
```

```python
import math
from contextlib import ExitStack

import concourse.bass as bass
import numpy as np
from concourse import mybir

F32 = mybir.dt.float32
F32R = mybir.dt.float32r
I32 = mybir.dt.int32
ALU = mybir.AluOpType
ACT = mybir.ActivationFunctionType
AX = mybir.AxisListType

P = 128
D = 2048
SEQ = 256
NSEQ, TOK = 8, 4
SAMP = NSEQ * TOK
ROWS = SEQ + SAMP
HEADS = 8
PAST = 256
PAGES = 2
FF = 5504
KT = D // P
FT = FF // P
BUCKETS, MAXDIST = 32, 1024
ALPHA = 2.0 ** 0.25
EPS = 1e-5
NEG = -1e30
SCALE = float(P) ** -0.5
UW = SEQ + 2 + NSEQ * (TOK + 2)
CW = UW - 2
TABLES = 1 + 4 * TOK
OUT_BANKS = (2, 3, 6, 7)
MODS = 9

SLAB = 2 * 4 * P
RING = 4
AHEAD = 3
IN_GROUPS, IN_STEPS = 10, 20
UP_GROUPS = [8, 8, 5]
S_IN = 0
S_OUT = S_IN + 4 * IN_STEPS
S_UP = [S_OUT + 32, S_OUT + 128, S_OUT + 224]
S_DN = [S_UP[0] + 64, S_UP[1] + 64, S_UP[2] + 48]


def slab_columns(s):
    tail = S_UP[2] + 40 <= s < S_DN[2] or (s >= S_DN[2] and (s - S_DN[2]) % 6 == 5)
    return SLAB // 2 if tail else SLAB


TD_IN, TD_OUT = 0, 3 * 40
TD_UP = [3 * 48, 3 * 60, 3 * 72]
TD_DN = [3 * 56, 3 * 68, 3 * 77 + 1]
GROUPS_BEFORE = [0, 8, 16]

ADA_STEPS = 16
ADA_PAIRS = [(1, 6), (2, 7), (3, 8)]
ADA_SINGLES = [9, 4, 5, 10, 11]
A_IN, A_LAST, A_GATE, A_UP = 16, 112, 128, 160
G1, SH2, SC2, G2 = 32, 48, 64, 80

V_ADA, V_G1, V_B1, V_NA, V_NB, V_G2, V_B2, V_CONV = 0, 96, 112, 128, 136, 144, 160, 176
V_ALL = V_CONV + 4 * 2 * FT
C_ID, C_TRI, C_M32, C_MP, C_MN, C_BD = 0, 128, 256, 512, 544, 576
C_ALL = 608
REL_MAX = PAST + TOK - 1
REL_N = REL_MAX + 1 + 127


def buckets(n):
    nf = np.maximum(n, 1).astype(np.float32)
    half = BUCKETS // 2
    large = half + (np.log(nf / np.float32(half)) / np.float32(math.log(MAXDIST / half)) * np.float32(half)).astype(np.int32)
    return np.where(n < half, n, np.minimum(large, BUCKETS - 1))


def shape_constants():
    c = np.zeros((P, C_ALL), np.float32)
    i = np.arange(P)
    c[:, C_ID:C_ID + P] = np.eye(P)
    c[:, C_TRI:C_TRI + P] = i[None, :] >= i[:, None]
    own = (np.arange(SAMP)[None, :] // TOK == np.arange(NSEQ)[:, None]).astype(np.float32)
    c[:, C_M32:C_M32 + NSEQ * SAMP] = own.reshape(1, -1)
    mine = (i[:, None] % SAMP) // TOK == np.arange(SAMP)[None, :] // TOK
    c[:, C_MP:C_MP + SAMP] = mine
    c[:, C_MN:C_MN + SAMP] = np.where(mine, 0.0, NEG)
    j = np.arange(SAMP)
    c[:SAMP, C_BD:C_BD + SAMP] = j[None, :] % TOK >= j[:, None] % TOK
    rel = REL_MAX - np.arange(REL_N)
    hot = np.zeros((BUCKETS + 1, REL_N), np.float32)
    hot[np.where(rel >= 0, buckets(np.maximum(rel, 0)), BUCKETS), np.arange(REL_N)] = 1.0
    return c, hot




SBUF_BYTES = 212000


class Steps:

    def __init__(self, eng, sem):
        self.eng, self.sem, self.n, self.it, self.per, self.start = eng, sem, 0, None, 0, 0

    def link(self, ins):
        self.n += 1
        ins.then_inc(self.sem, 1)
        self.eng.wait_ge(self.sem, self.n if self.it is None else self.it * self.per + self.n)

    def enter(self, it, per):
        self.it, self.per, self.start = it, per, self.n

    def leave(self, iterations):
        assert self.n - self.start == self.per, (self.n - self.start, self.per)
        self.n += self.per * (iterations - 1)
        self.it = None


def decoder_layer_program(nc, io, n_phys):
    with ExitStack() as ctx:
        base = (nc.sbuf_base + 31) // 32 * 32
        ctx.enter_context(nc.sbuf_tensor("arena", [P, SBUF_BYTES // 4], F32))
        top = 0

        def place(name, shape, dt=F32, over=None):
            nonlocal top
            size = (4 * int(np.prod(shape[1:])) + 31) // 32 * 32
            offset = top if over is None else over
            if over is None:
                top += size
            assert offset + size <= SBUF_BYTES - 32, (name, offset + size)
            return nc.alloc_sbuf_tensor_at(name, shape, dt, offset=base + offset), offset

        T = KT * ROWS
        xT, _ = place("xT", [P, T])
        hH, o_h = place("hH", [P, T], F32R)
        hL, _ = place("hL", [P, T], F32R)
        modT, _ = place("modT", [P, 96 * MODS])
        vec, _ = place("vec", [P, V_ALL])
        cst, _ = place("cst", [P, C_ALL])
        ones, _ = place("ones", [P, P])
        cT, _ = place("cT", [P, KT * 32])
        raw, _ = place("raw", [P, RING * SLAB])
        wH, _ = place("wH", [P, RING * SLAB], F32R)
        wL, _ = place("wL", [P, RING * SLAB], F32R)
        ada, _ = place("ada", [P, RING * 1024])
        adaS, _ = place("adaS", [P, 512])
        past, o_past = place("past", [P, 2 * FT * 16])
        wsT, o_ws = place("wsT", [P, HEADS * P])
        bd, o_bd = place("bd", [SAMP, HEADS * SAMP])
        small, _ = place("small", [P, 160])
        cw, _ = place("cw", [P, 16])
        pages, _ = place("pages", [1, 16], I32)
        S4, o_s4 = place("S4", [P, 4 * ROWS])
        RN, _ = place("RN", [P, 2 * ROWS], over=o_s4)
        region = top
        proj, o_proj = place("proj", [P, 40 * ROWS])
        o_va = o_proj + 4 * 32 * ROWS
        Vrm, o_v = place("Vrm", [P, 2 * 1024])
        Vn, o_vn = place("Vn", [SAMP, 1024])
        VAs, o_vas = place("VAs", [SAMP, 1024])
        mix, _ = place("mix", [P, 32 * ROWS], F32R, over=o_proj)
        H32, _ = place("H32", [P, 4 * ROWS], over=o_v)
        hot, _ = place("hot", [BUCKETS + 1, REL_N], over=o_vn)
        rbias, _ = place("rbias", [BUCKETS + 1, HEADS], over=o_vn + 1568)
        bvec, _ = place("bvec", [HEADS, 2 * REL_N], over=o_vn + 1632)
        RR, _ = place("RR", [P, 2 * ROWS], over=o_vas)
        VA, _ = place("VA", [P, 2 * 1024], over=o_va)
        Tm, _ = place("Tm", [P, 2 * 512], over=o_s4)
        Lp, _ = place("Lp", [P, 2 * 384], over=o_va)
        Pp, _ = place("Pp", [P, 2 * 384], over=o_va + 3072)
        PTp, _ = place("PTp", [P, 2 * 384], over=o_va + 6144)
        TB, _ = place("TB", [P, HEADS * 256], over=o_h)
        BS, _ = place("BS", [P, 1024], over=o_h + 8192)
        Ls, _ = place("Ls", [P, 2 * ROWS], over=o_h + 8192)
        SBi, _ = place("SBi", [P, 2 * ROWS], over=o_h + 12288)
        E4, _ = place("E4", [P, 2 * TOK], over=o_h + 14592)
        Qm, _ = place("Qm", [P, 2 * 256], over=o_h + 14624)
        PTs, _ = place("PTs", [P, 4 * P], over=o_h + 16672)
        PN, _ = place("PN", [SAMP, 2 * P], over=o_h + 18720)
        KV, _ = place("KV", [P, 2 * 2048], over=o_h + 20480)
        SG, _ = place("SG", [P, 1024], over=o_s4)
        SH, _ = place("SH", [P, 1024], over=o_past)
        PTm, _ = place("PTm", [P, 2 * 512], over=o_ws)
        OS, _ = place("OS", [P, 2 * P], over=o_bd)
        top = region
        ffH, _ = place("ffH", [P, 16 * ROWS], F32R)
        ffL, _ = place("ffL", [P, 16 * ROWS], F32R)
        U, _ = place("U", [P, 4 * UW])
        CV, o_cv = place("CV", [P, 4 * CW])
        SA, o_sa = place("SA", [P, 2 * CW])
        Ff, _ = place("Ff", [P, 2 * ROWS])
        E, _ = place("E", [P, 2 * FT * 18])
        DG, _ = place("DG", [P, 6 * P], over=o_cv)
        H2, _ = place("H2", [P, 4 * ROWS], over=o_sa)

        ps = ctx.enter_context(nc.psum_tensor("ps", [P, 8, 512], F32))
        bias_rows = nc.dram_tensor("bias_rows", [2 * HEADS, REL_N], F32, kind="Internal").ap()
        ident = cst[:, C_ID:C_ID + P]

        def sem(name):
            return ctx.enter_context(nc.semaphore(name))

        raw_in = [sem(f"raw_in{i}") for i in range(RING)]
        ada_in = [sem(f"ada_in{i}") for i in range(RING)]
        hi_done = sem("hi_done")
        split_done = sem("split_done")
        used = sem("used")
        tile_done = sem("tile_done")
        ada_used = sem("ada_used")
        bank_full = [sem(f"bank_full{i}") for i in range(8)]
        bank_free = [sem(f"bank_free{i}") for i in range(8)]
        dve_step = sem("dve_step")
        small_in, bias_in, gate_in, past_in = sem("small_in"), sem("bias_in"), sem("gate_in"), sem("past_in")
        x_in, x_rest_in, c_in = sem("x_in"), sem("x_rest_in"), sem("c_in")
        c_silu, proj_zeroed = sem("c_silu"), sem("proj_zeroed")
        adaS_ready = sem("adaS_ready")
        h32_ready, hH_ready, h_ready = sem("h32_ready"), sem("hH_ready"), sem("h_ready")
        proj_ready, gelu_ready = sem("proj_ready"), sem("gelu_ready")
        bvec_stored = sem("bvec_stored")
        sgu_in, table_in = sem("sgu_in"), sem("table_in")
        var_ready, va_sd, va_ready, gm_ready = sem("var_ready"), sem("va_sd"), sem("va_ready"), sem("gm_ready")
        logit_ready, exp_ready, prob_ready = sem("logit_ready"), sem("exp_ready"), sem("prob_ready")
        kv_in, kv_used = [sem("kv_in0"), sem("kv_in1")], sem("kv_used")
        qm_ready, ptm_ready, pages_in, tails_stored = sem("qm_ready"), sem("ptm_ready"), sem("pages_in"), sem("tails_stored")
        s_logit, s_exp, s_prob = sem("s_logit"), sem("s_exp"), sem("s_prob")
        sq_ready, m_ready, mH_ready, m_split = (
            sem("sq_ready"), sem("m_ready"), sem("mH_ready"), sem("m_split"))
        s4_ready, s4_copied = sem("s4_ready"), sem("s4_copied")
        last_scaled, last_centred = sem("last_scaled"), sem("last_centred")
        ln_var, ln_sd, diag_ready = sem("ln_var"), sem("ln_sd"), sem("diag_ready")
        xn_ready, x1_ready = sem("xn_ready"), sem("x1_ready")
        h2_prompt, h2_32, h2H, h2_ready = sem("h2_prompt"), sem("h2_32"), sem("h2H"), sem("h2_ready")
        pads_set, past_ready, tails_ready = sem("pads_set"), sem("past_ready"), sem("tails_ready")
        conv_ready, silu_ready, ff32_ready, ffH_ready, ff_ready = (
            sem("conv_ready"), sem("silu_ready"), sem("ff32_ready"), sem("ffH_ready"), sem("ff_ready"))
        kv_stored, va_stored, stored = sem("kv_stored"), sem("va_stored"), sem("stored")

        taken, done = [1] * 5 + [0] * 3, [0] * 8
        JOBS = {}

        def take(pe, job, bank, it=0, per=0):
            if taken[bank]:
                pe.wait_ge(bank_free[bank], taken[bank] + it * per)
            JOBS[job] = (bank, done[bank], taken[bank], per)
            taken[bank] += 1
            return ps[:, bank, :]

        def fill(ins, job):
            done[JOBS[job][0]] += 1
            ins.then_inc(bank_full[JOBS[job][0]], 1)

        def filled(eng, job, it=0):
            bank, n, _, per = JOBS[job]
            eng.wait_ge(bank_full[bank], n + 1 + it * per)
            return ps[:, bank, :]

        def release(ins, job):
            ins.then_inc(bank_free[JOBS[job][0]], 1)

        def released(eng, job, it=0):
            bank, _, n, per = JOBS[job]
            eng.wait_ge(bank_free[bank], n + 1 + it * per)

        def tile(t, k, lo=0, hi=ROWS):
            return t[:, k * ROWS + lo:k * ROWS + hi]

        def tiles(t, k, n, lo=0, hi=ROWS):
            if isinstance(k, int):
                v = t[:, k * ROWS:(k + n) * ROWS]
            else:
                v = t[:, bass.ds(k * ROWS, n * ROWS)]
            return v.rearrange("p (k c) -> p k c", k=n)[:, :, lo:hi]

        def spread(ap, *dims):
            return bass.AP(ap.tensor, ap.offset, [list(ap.ap[0])] + [list(d) for d in dims])

        def mods(k, n):
            if isinstance(k, int):
                v = modT[:, k * MODS:(k + n) * MODS]
            else:
                v = modT[:, bass.ds(k * MODS, n * MODS)]
            return (spread(v, [MODS, n], [0, SEQ]),
                    spread(v.rearrange("p (k c) -> p k c", k=n)[:, :, 1:MODS], [MODS, n], [1, NSEQ], [0, TOK]))

        def by_seq(v, n):
            return v.rearrange("p k (n t) -> p k n t", t=TOK)

        def mix_hi(k):
            return tile(mix, 16 + k if k < 8 else k)

        def mix_lo(k):
            return tile(mix, 24 + k if k < 8 else k - 8)

        def mixed(k):
            return tile(proj, 24 + k if k < 8 else k - 8)

        block = ctx.enter_context(nc.Block())

        @block.tensor
        def _(pe):
            def products(s, i, rhs_hi, rhs_lo, banks, first, last, ktiles=2, taking=None):
                pe.wait_ge(split_done, s + 1)
                n = len(banks)
                for kk in range(ktiles):
                    for t in range(n):
                        w = (i % RING) * SLAB + (kk * n + t) * P
                        start, stop = first and kk == 0, last and kk == ktiles - 1
                        if start:
                            taking(t)
                        out = ps[:, banks[t], 0:ROWS]
                        nc.tensor.matmul(out, wH[:, w:w + P], rhs_lo(kk), start=start, stop=False)
                        nc.tensor.matmul(out, wL[:, w:w + P], rhs_hi(kk), start=False, stop=False)
                        mm = nc.tensor.matmul(out, wH[:, w:w + P], rhs_hi(kk), start=False, stop=stop)
                        if kk == ktiles - 1 and t == n - 1:
                            mm.then_inc(used, 1)
                        elif stop:
                            mm.then_inc(tile_done, 1)

            def ada_slab(a, slot, turn, k, copies, bank=6):
                if k == 0 and not (isinstance(copies, int) and copies == 0):
                    pe.wait_ge(adaS_ready, copies)
                pe.wait_ge(ada_in[slot], turn * 16 + 16)
                for c in range(4):
                    o = slot * 1024 + 256 * c
                    mm = nc.tensor.matmul(ps[32 * c:32 * c + 32, bank, 0:256], cT[:, 32 * k:32 * k + 32],
                                          ada[:, o:o + 256], start=(k == 0), stop=(k == ADA_STEPS - 1))
                mm.then_inc(ada_used, 1)

            def ada_turn(copies, job, it=0, per=0, parts=1, bank=7):
                pe.wait_ge(adaS_ready, copies + 1)
                b = take(pe, job, bank, it, per)
                for j in range(2 * parts):
                    mm = nc.tensor.transpose(b[:, j * P:(j + 1) * P], adaS[:, j * P:(j + 1) * P], ident)
                fill(mm, job)

            pe.wait_ge(small_in, 16 * 2)
            pe.wait_ge(bias_in, 32)
            b = take(pe, "bias", 5)
            fill(nc.tensor.matmul(b[0:HEADS, 0:REL_N], rbias[:, :], hot[:, :], start=True, stop=True), "bias")
            pe.wait_ge(c_silu, 1)
            for k in range(ADA_STEPS):
                ada_slab(k, k % RING, k // RING, k, 0)
            ada_turn(0, ("turn", 0))

            def w_in_quarter(kg, it, loop):
                pe.wait_ge(h_ready, kg + 1)
                for i in range(IN_STEPS):
                    g, half = divmod(i, 2)
                    banks = [(4 * g + t) % 5 for t in range(4)]

                    def rhs(src):
                        def at(kk):
                            if loop:
                                return src[:, bass.ds((kg * 4 + 2 * half + kk) * ROWS, ROWS)]
                            return tile(src, kg * 4 + 2 * half + kk)
                        return at
                    products(kg * IN_STEPS + i, i, rhs(hH), rhs(hL), banks, half == 0, half == 1,
                             taking=lambda t: take(pe, ("in", loop, 4 * g + t), banks[t], it, 8))
                    if i < ADA_STEPS:
                        if loop:
                            for part in range(2):
                                a = 2 * i + part
                                ada_slab(kg * 32 + (A_IN + a), a % RING, kg * 8 + (A_IN + a) // RING, i, kg + 1, 5 + part)
                        else:
                            ada_slab(A_LAST + i, i % RING, (A_LAST + i) // RING, i, 4)
                    if i == ADA_STEPS:
                        ada_turn(kg + 1, ("turn in", loop), it, 1, parts=2 if loop else 1)

            with pe.Fori(0, 3) as kg:
                w_in_quarter(kg, kg, True)
            for bank in range(5):
                taken[bank] += 2 * 8
            taken[7] += 2
            done[7] += 2
            w_in_quarter(3, 0, False)

            def ada_slabs(unit, first, last):
                for k in range(first, last):
                    a = A_GATE + ADA_STEPS * (unit - 4) + k
                    ada_slab(a, k % RING, a // RING, k, unit + 1, 6 if unit == 4 else 5)

            pe.wait_ge(proj_ready, 1)
            for hg in range(2):
                for r in range(3):
                    job, n = ("v", r, hg), P if r < 2 else SAMP
                    b = take(pe, job, 3 * hg + r)
                    for h in range(4):
                        mm = nc.tensor.transpose(b[0:n, h * P:(h + 1) * P], tile(proj, 16 + 4 * hg + h, r * P, r * P + n), ident)
                    fill(mm, job)
            pe.wait_ge(gelu_ready, 1)
            for r in range(3):
                for hg in range(2):
                    job, n = ("va", r, hg), P if r < 2 else SAMP
                    b = take(pe, job, 3 * hg + r)
                    for h in range(4):
                        mm = nc.tensor.transpose(b[0:n, h * P:(h + 1) * P], tile(proj, 32 + 4 * hg + h, r * P, r * P + n), ident)
                    fill(mm, job)
                    ada_slabs(4, 2 * r + hg, 2 * r + hg + 1)
            for c in range(2):
                pe.wait_ge(va_ready, c + 1)
                for gg in range(2):
                    job = ("gate", c, gg)
                    b = take(pe, job, 2 * c + gg)
                    for g in range(4 * gg, 4 * gg + 4):
                        mm = nc.tensor.matmul(b[:, (g % 4) * P:(g % 4 + 1) * P], VA[:, c * 1024 + g * P:c * 1024 + (g + 1) * P],
                                              wsT[:, g * P:(g + 1) * P], start=True, stop=True)
                    fill(mm, job)
                    ada_slabs(4, 6 + 4 * c + 2 * gg, 8 + 4 * c + 2 * gg)
            pe.wait_ge(va_ready, 3)
            b = take(pe, "gate decode", 4)
            for g in range(HEADS):
                mm = nc.tensor.matmul(b[:, g * SAMP:(g + 1) * SAMP], VAs[0:SAMP, g * P:(g + 1) * P],
                                      bd[0:SAMP, g * SAMP:(g + 1) * SAMP], start=True, stop=True)
            fill(mm, "gate decode")
            ada_slabs(4, 14, 16)
            ada_turn(5, ("turn", 4))

            b = take(pe, "S new", 3)
            for h in range(HEADS):
                hh, hq = divmod(h, 4)
                mm = nc.tensor.matmul(b[32 * hq:32 * hq + 32, hh * SAMP:(hh + 1) * SAMP], tile(proj, h, SEQ, ROWS),
                                      tile(proj, 8 + h, SEQ, ROWS), start=True, stop=True)
            fill(mm, "S new")
            take(pe, "S past 0", 6)
            take(pe, "S past 1", 7)

            def scores(h):
                b = take(pe, ("S", h), h % 2)
                q, k = lambda lo, hi: tile(proj, h, lo, hi), lambda lo, hi: tile(proj, 8 + h, lo, hi)
                nc.tensor.matmul(b[:, 0:P], q(0, P), k(0, P), start=True, stop=True)
                fill(nc.tensor.matmul(b[:, P:3 * P], q(P, 2 * P), k(0, 2 * P), start=True, stop=True), ("S", h))

            def past_scores(n):
                pe.wait_ge(kv_in[n % 2], 32 * (n // 2 + 1))
                pe.wait_ge(qm_ready, n + 1)
                for h in range(HEADS):
                    hh, hq = divmod(h, 4)
                    keys = KV[:, (n % 2) * 2048:(n % 2 + 1) * 2048].rearrange("p (g h c) -> p g h c", g=PAGES, h=HEADS)[:, :, h, :]
                    mm = nc.tensor.matmul(ps[32 * hq:32 * hq + 32, 6 + hh, 0:PAST], Qm[:, (n % 2) * 256 + h * 32:(n % 2) * 256 + (h + 1) * 32],
                                          keys, start=(n == 0), stop=(n == NSEQ - 1))
                mm.then_inc(kv_used, 1)

            def sum_squares(a, bank):
                pe.wait_ge(sq_ready, a + 1)
                job, k0 = ("sum a", 16) if a == 0 else ("sum b", 8)
                b = take(pe, job, bank)
                for k in range(8):
                    mm = nc.tensor.matmul(b[:, 0:ROWS], ones[:, :], tile(proj, k0 + k), start=(k == 0), stop=(k == 7))
                fill(mm, job)

            scores(0)
            for h in range(HEADS):
                if h + 1 < HEADS:
                    scores(h + 1)
                if h == 1:
                    sum_squares(0, 4)
                past_scores(h)
                ada_slabs(5, h, h + 1)
                pe.wait_ge(prob_ready, h + 1)
                b = take(pe, ("PT", h), 2 + h % 2)
                for j in range(3):
                    o = (h % 2) * 384 + j * P
                    mm = nc.tensor.transpose(b[:, j * P:(j + 1) * P], Pp[:, o:o + P], ident)
                fill(mm, ("PT", h))
                b = take(pe, ("PV", h), 4)
                released(pe, ("PT", h))
                o = (h % 2) * 384
                nc.tensor.matmul(b[:, 0:2 * P], Vrm[:, h * P:(h + 1) * P], PTp[:, o:o + 2 * P], start=True, stop=False)
                fill(nc.tensor.matmul(b[:, P:2 * P], Vrm[:, 1024 + h * P:1024 + (h + 1) * P], PTp[:, o + 2 * P:o + 3 * P],
                                      start=False, stop=True), ("PV", h))

            def out_slabs(first, last):
                for n in range(first, last):
                    g, j = divmod(n, 4)
                    if g == 0:
                        pe.wait_ge(m_split, 2 * j + 2)
                    products(S_OUT + n, n, lambda kk: mix_hi(2 * j + kk), lambda kk: mix_lo(2 * j + kk), OUT_BANKS, j == 0, j == 3,
                             taking=lambda t: take(pe, ("out a", g, t), OUT_BANKS[t]))

            out_slabs(0, 2)
            pe.wait_ge(s_prob, 1)
            b = take(pe, "s PT", 4)
            for hh in range(2):
                for kt in range(2):
                    mm = nc.tensor.transpose(b[:, (2 * hh + kt) * P:(2 * hh + kt + 1) * P], Ls[:, hh * ROWS + kt * P:hh * ROWS + (kt + 1) * P], ident)
            fill(mm, "s PT")
            b = take(pe, "s PN", 4)
            for hh in range(2):
                mm = nc.tensor.transpose(b[0:SAMP, hh * P:(hh + 1) * P], Ls[:, hh * ROWS + PAST:(hh + 1) * ROWS], ident)
            fill(mm, "s PN")
            take(pe, "O 0", 0)
            take(pe, "O 1", 1)
            for n in range(NSEQ):
                pe.wait_ge(kv_in[n % 2], 32 * (4 + n // 2 + 1))
                pe.wait_ge(ptm_ready, n + 1)
                for kt in range(2):
                    for h in range(HEADS):
                        hh, hq = divmod(h, 4)
                        o = (n % 2) * 512 + ((2 * hh + kt) * 4 + hq) * 32
                        mm = nc.tensor.matmul(ps[32 * hq:32 * hq + 32, hh, 0:P], PTm[:, o:o + 32],
                                              KV[:, (n % 2) * 2048 + kt * 1024 + h * P:(n % 2) * 2048 + kt * 1024 + (h + 1) * P],
                                              start=(n == 0 and kt == 0), stop=False)
                mm.then_inc(kv_used, 1)
                ada_slabs(5, 8 + n, 9 + n)
                if n:
                    out_slabs(1 + n, 2 + n)
            released(pe, "s PN")
            for h in range(HEADS):
                hh, hq = divmod(h, 4)
                mm = nc.tensor.matmul(ps[32 * hq:32 * hq + 32, hh, 0:P], PN[0:SAMP, hh * P + 32 * hq:hh * P + 32 * hq + 32],
                                      Vn[0:SAMP, h * P:(h + 1) * P], start=False, stop=True)
                if h == 3:
                    fill(mm, "O 0")
            fill(mm, "O 1")
            ada_turn(6, ("turn", 5), bank=4)
            out_slabs(9, 11)
            released(pe, "O 0")
            released(pe, "O 1")
            b = take(pe, "OT", 5)
            nc.tensor.transpose(b[:, 0:P], OS[:, 0:P], ident)
            fill(nc.tensor.transpose(b[:, P:2 * P], OS[:, P:2 * P], ident), "OT")
            out_slabs(11, 13)
            sum_squares(1, 5)
            out_slabs(13, 16)

            def turn_rows(g, ln):
                pe.wait_ge(s4_ready, 4 * ln + g + 1)
                for r, bank in enumerate((4, 5, 7)):
                    n = P if r < 2 else SAMP
                    b = take(pe, ("rows", ln, g, r), bank)
                    for t in range(4):
                        mm = nc.tensor.transpose(b[0:n, t * P:(t + 1) * P], tile(S4, t, r * P, r * P + n), ident)
                    fill(mm, ("rows", ln, g, r))

            def spread_rows(ln):
                pe.wait_ge(diag_ready, ln + 1)
                for j in range(2):
                    b = take(pe, ("ln", ln, j), 4 + j)
                    for r in range(3):
                        n = P if r < 2 else SAMP
                        mm = nc.tensor.matmul(b[:, r * P:r * P + n], ones[0:n, :], DG[0:n, (2 * r + j) * P:(2 * r + j) * P + n],
                                              start=True, stop=True)
                    fill(mm, ("ln", ln, j))

            for g in range(4):
                for j in range(4):
                    if g == 0:
                        pe.wait_ge(m_split, 8 + 2 * j + 2)
                    products(S_OUT + 16 + 4 * g + j, j, lambda kk: mix_hi(8 + 2 * j + kk), lambda kk: mix_lo(8 + 2 * j + kk),
                             range(4), j == 0, j == 3, taking=lambda t: take(pe, ("out", g, t), t))
                    if g and j == 1:
                        turn_rows(g - 1, 0)
            turn_rows(3, 0)
            spread_rows(0)

            def up_group(s, i0, job, it, per, halves=2, units=None):
                banks = [0, 1, 2, 3] if halves == 2 else [0, 2]
                for j in range(8):
                    pe.wait_ge(h2_ready, j // 2 + 1)
                    products(s + j, i0 + j, lambda kk: tile(hH, 2 * j + kk), lambda kk: tile(hL, 2 * j + kk),
                             banks, j == 0, j == 7, taking=lambda t: take(pe, (job, banks[t]), banks[t], it, per))
                    if units is not None:
                        k = i0 + j
                        ada_slab(units * 16 + (A_UP + k), k % RING, units * 4 + (A_UP + k) // RING, k, units + 7)

            def after_loop(banks, per, iterations):
                for bank in banks:
                    taken[bank] += per * (iterations - 1)

            for ph in range(3):
                if ph == 0:
                    with pe.Fori(0, 2) as u:
                        up_group(u * 16 + S_UP[0], 0, ("up", 0, "a"), u, 2, units=u)
                        up_group(u * 16 + S_UP[0] + 8, 8, ("up", 0, "b"), u, 2, units=u)
                        ada_turn(u + 7, ("turn up",), u, 1)
                    after_loop(range(4), 2, 2)
                    after_loop([7], 1, 2)
                    done[7] += 1
                    with pe.Fori(0, 4) as g:
                        up_group(g * 8 + S_UP[0] + 32, 0, ("up", 0, "c"), g, 1)
                    after_loop(range(4), 1, 4)
                else:
                    with pe.Fori(0, UP_GROUPS[ph]) as g:
                        up_group(g * 8 + S_UP[ph], 0, ("up", ph), g, 1)
                    after_loop(range(4), 1, UP_GROUPS[ph])
                if ph == 2:
                    up_group(S_UP[2] + 40, 0, ("up tail",), 0, 0, halves=1)
                if ph < 2:
                    with pe.Fori(0, 4) as g:
                        for j in range(8):
                            pe.wait_ge(ff_ready, GROUPS_BEFORE[ph] + j + 1)
                            products(g * 8 + S_DN[ph] + j, j, lambda kk: tile(ffH, 2 * j + kk), lambda kk: tile(ffL, 2 * j + kk),
                                     range(4), j == 0, j == 7, taking=lambda t: take(pe, ("down", ph, t), t, g, 1))
                    after_loop(range(4), 1, 4)
                else:
                    for g in range(4):
                        for j in range(6):
                            if g == 0:
                                pe.wait_ge(ff_ready, GROUPS_BEFORE[2] + j + 1)
                            products(S_DN[2] + 6 * g + j, 6 * g + j, lambda kk: tile(ffH, 2 * j + kk),
                                     lambda kk: tile(ffL, 2 * j + kk), range(4), j == 0, j == 5, ktiles=2 if j < 5 else 1,
                                     taking=lambda t: take(pe, ("down", 2, g, t), t))
                            if g and j == 2:
                                turn_rows(g - 1, 1)
                    turn_rows(3, 1)
                    spread_rows(1)

        @block.sync
        def _(sp):
            def load(s, source, index, slot, cols=SLAB):
                if not isinstance(s, int) or s >= RING:
                    sp.wait_ge(split_done, s - RING + 1)
                src = source[bass.ds(index, 1), :, :].rearrange("a p c -> (a p) c") if not isinstance(index, int) else source[index, :, :]
                sp.dma_start(raw[:, slot * SLAB:slot * SLAB + cols], src).then_inc(raw_in[slot], 16)

            def load_ada(a, slot):
                if not isinstance(a, int) or a >= RING:
                    sp.wait_ge(ada_used, a - RING + 1)
                src = io["w_ada"][bass.ds(a, 1), :, :].rearrange("a p c -> (a p) c") if not isinstance(a, int) else io["w_ada"][a, :, :]
                sp.dma_start(ada[:, slot * 1024:(slot + 1) * 1024], src).then_inc(ada_in[slot], 16)

            for k in range(ADA_STEPS):
                if k >= 13:
                    load(k - 13, io["w_in"], k - 13, k - 13)
                load_ada(k, k % RING)
            load(AHEAD, io["w_in"], AHEAD, AHEAD)
            with sp.Fori(0, 3) as kg:
                for i in range(1, IN_STEPS + 1):
                    if i <= ADA_STEPS:
                        for a in (2 * i - 2, 2 * i - 1):
                            load_ada(kg * 32 + (A_IN + a), a % RING)
                    s = kg * IN_STEPS + (i + AHEAD)
                    load(s, io["w_in"], s, (i + AHEAD) % RING)
            for i in range(1, IN_STEPS + 1):
                if i <= ADA_STEPS:
                    load_ada(A_LAST + i - 1, (i - 1) % RING)
                s = 3 * IN_STEPS + i + AHEAD
                if s < S_OUT:
                    load(s, io["w_in"], s, s % RING)
                else:
                    load(s, io["w_out"], s - S_OUT, s % RING)
            for k in range(24):
                load_ada(A_GATE + k, k % RING)
            for s in range(S_OUT + 4, S_UP[0]):
                if s < S_OUT + 12:
                    load_ada(A_GATE + 20 + s - S_OUT, s % RING)
                load(s, io["w_out"], s - S_OUT, s % RING)
            for j in range(3):
                load(S_UP[0] + j, io["w_up"], j, j)
            with sp.Fori(0, 2) as u:
                for i in range(16):
                    load(u * 16 + (S_UP[0] + i + AHEAD), io["w_up"], u * 16 + (i + AHEAD), (i + AHEAD) % RING)
                    load_ada(u * 16 + (A_UP + i), i % RING)

            def stream(s0, source, index0, n):
                with sp.Fori(0, n // 4) as m:
                    for j in range(4):
                        load(m * 4 + (s0 + j), source, m * 4 + (index0 + j), (s0 + j) % RING)
                for j in range(n // 4 * 4, n):
                    load(s0 + j, source, index0 + j, (s0 + j) % RING)

            stream(S_UP[0] + 35, io["w_up"], 35, 29)
            stream(S_DN[0], io["w_down"], 0, 32)
            stream(S_UP[1], io["w_up"], 64, 64)
            stream(S_DN[1], io["w_down"], 32, 32)
            stream(S_UP[2], io["w_up"], 128, 40)
            for j in range(8):
                load(S_UP[2] + 40 + j, io["w_up_tail"], j, j % RING, SLAB // 2)
            for g in range(4):
                for j in range(6):
                    s = S_DN[2] + 6 * g + j
                    if j < 5:
                        load(s, io["w_down"], 64 + 5 * g + j, s % RING)
                    else:
                        load(s, io["w_down_tail"], g, s % RING, SLAB // 2)

        @block.scalar
        def _(act):
            def eps_col(i):
                return small[:, 140 + i:141 + i]

            def hi(s, n4, slot, cols=SLAB):
                act.wait_ge(raw_in[slot], n4 * 16 + 16)
                if not isinstance(s, int) or s >= RING:
                    act.wait_ge(used, s - RING + 1)
                o = slot * SLAB
                nc.scalar.activation(wH[:, o:o + cols], raw[:, o:o + cols], ACT.Copy).then_inc(hi_done, 1)

            def hi_ahead(s0, n0, i):
                j = i + AHEAD
                hi(s0 + j, n0 + j // RING, j % RING)

            def ada_copy(copies, upto, parts=1, bank=6, turned=None):
                act.wait_ge(ada_used, upto)
                if not isinstance(copies, int) or copies > 0:
                    act.wait_ge(bank_full[7], copies if turned is None else turned)
                nc.scalar.activation(adaS[:, 0:256 * parts].rearrange("p (a c) -> p a c", a=parts), ps[:, bank + 1 - parts:bank + 1, 0:256], ACT.Copy).then_inc(adaS_ready, 1)

            def h_hi(kg):
                act.wait_ge(h32_ready, kg + 1)
                nc.scalar.activation(tiles(hH, kg * 4, 4), tiles(H32, 0, 4), ACT.Copy).then_inc(hH_ready, 1)

            act.dma_start(cT[:, :], io["cT"][:, :]).then_inc(c_in, 16)
            act.dma_start(xT[:, 0:4 * ROWS], io["xT"][:, 0:4 * ROWS]).then_inc(x_in, 16)
            act.wait_ge(c_in, 16)
            nc.scalar.activation(cT[:, :], cT[:, :], ACT.Silu).then_inc(c_silu, 1)
            for s in range(AHEAD):
                hi(s, 0, s)
            act.dma_start(xT[:, 4 * ROWS:], io["xT"][:, 4 * ROWS:]).then_inc(x_rest_in, 16)
            ada_copy(0, A_IN)
            h_hi(0)
            hi_ahead(0, 0, 0)
            with act.Fori(0, 3) as kg:
                for i in range(1, IN_STEPS + 1):
                    hi_ahead(kg * IN_STEPS, kg * 5, i)
                    if i == ADA_STEPS + 1:
                        h_hi(kg + 1)
                    if i == ADA_STEPS:
                        ada_copy(kg + 1, kg * 32 + (A_IN + 32), parts=2)
            for i in range(1, IN_STEPS + 1):
                hi_ahead(3 * IN_STEPS, 15, i)
                if i == ADA_STEPS:
                    ada_copy(4, A_GATE)

            act.wait_ge(proj_ready, 1)
            for k in (32, 24):
                v = proj[:, k * ROWS:(k + 8) * ROWS]
                nc.scalar.activation(v, v, ACT.Gelu_apprx_tanh).then_inc(gelu_ready, 1)
            for hg in range(2):
                for r in range(2):
                    b = filled(act, ("v", r, hg))
                    release(nc.scalar.activation(Vrm[:, r * 1024 + hg * 512:r * 1024 + (hg + 1) * 512], b, ACT.Copy), ("v", r, hg))
            act.wait_ge(var_ready, 3)
            nc.scalar.activation(small[:, 42:45], spread(small[:, 37:38], [2, 3]), ACT.Sqrt, bias=eps_col(0)).then_inc(va_sd, 1)
            act.wait_ge(gm_ready, 1)
            act.wait_ge(kv_stored, 16)
            nc.scalar.activation(tiles(proj, 16, 8), tiles(proj, 24, 8), ACT.Square).then_inc(sq_ready, 1)

            def root(a):
                job = ("sum a", "sum b")[a]
                b = filled(act, job)
                release(nc.scalar.activation(RR[:, a * ROWS:(a + 1) * ROWS], b[:, 0:ROWS], ACT.Sqrt, scale=1.0 / 1024, bias=eps_col(0)), job)

            def mix_hi_at(k):
                act.wait_ge(m_ready, k // 4 + 1)
                nc.scalar.activation(mix_hi(k), mixed(k), ACT.Copy, scale=vec[:, V_NA + k:V_NA + k + 1]).then_inc(mH_ready, 1)

            ada_copy(5, A_GATE + 16)
            act.wait_ge(va_stored, 16)
            for h in range(HEADS + 1):
                if h < HEADS:
                    act.wait_ge(logit_ready, h + 1)
                    o = (h % 2) * 384
                    nc.scalar.activation(Pp[:, o:o + P], Lp[:, o:o + P], ACT.Exp, bias=small[:, 50 + 2 * (h % 2):51 + 2 * (h % 2)],
                                         accum_out=small[:, 54 + 2 * (h % 2):55 + 2 * (h % 2)])
                    nc.scalar.activation(Pp[:, o + P:o + 384], Lp[:, o + P:o + 384], ACT.Exp, bias=small[:, 51 + 2 * (h % 2):52 + 2 * (h % 2)],
                                         accum_out=small[:, 55 + 2 * (h % 2):56 + 2 * (h % 2)]).then_inc(exp_ready, 1)
                if h:
                    g = h - 1
                    b = filled(act, ("PT", g))
                    o = (g % 2) * 384
                    release(nc.scalar.activation(PTp[:, o:o + 384], b[:, 0:384], ACT.Copy), ("PT", g))
                    b = filled(act, ("PV", g))
                    release(nc.scalar.activation(tile(proj, g, 0, SEQ), b[:, 0:SEQ], ACT.Copy), ("PV", g))
                if h == 1:
                    root(0)
                if 4 <= h < 8:
                    mix_hi_at(2 * h - 8)
                    mix_hi_at(2 * h - 7)

            def out_step(n):
                hi_ahead(S_OUT, S_OUT // 4, n)

            act.wait_ge(s_logit, 1)
            for hh in range(2):
                e = nc.scalar.activation(Ls[:, hh * ROWS:(hh + 1) * ROWS], Ls[:, hh * ROWS:(hh + 1) * ROWS], ACT.Exp,
                                         bias=small[:, 58 + hh:59 + hh], accum_out=small[:, 60 + hh:61 + hh])
            e.then_inc(s_exp, 1)
            out_step(1)
            out_step(2)
            b = filled(act, "s PT")
            release(nc.scalar.activation(PTs[:, :], b, ACT.Copy), "s PT")
            for n in range(3, 12):
                out_step(n)
                if n == 9:
                    ada_copy(6, A_UP, bank=5)
            b = filled(act, "OT")
            release(nc.scalar.activation(tiles(proj, 0, 8, SEQ, ROWS), b[:, 0:256].rearrange("p (h c) -> p h c", h=8), ACT.Copy), "OT")
            released(act, "OT")
            nc.scalar.activation(tiles(proj, 8, 8), tiles(proj, 0, 8), ACT.Square).then_inc(sq_ready, 1)
            out_step(12)
            out_step(13)
            root(1)
            for k in range(8, 12):
                mix_hi_at(k)
            out_step(14)
            for k in range(12, 16):
                mix_hi_at(k)
            out_step(15)
            out_step(16)

            def copy_sum(g, ln):
                act.wait_ge(s4_ready, 4 * ln + g + 1)
                nc.scalar.activation(tiles(xT, 4 * g, 4), tiles(S4, 0, 4), ACT.Copy).then_inc(s4_copied, 1)

            for g in range(4):
                for j in range(1, 5):
                    out_step(16 + 4 * g + j)
                    if g and j == 1:
                        copy_sum(g - 1, 0)

            def normalise(ln, scale_at, bias_at):
                copy_sum(3, ln)
                act.wait_ge(ln_var, ln + 1)
                nc.scalar.activation(small[:, 130:133], small[:, 126:129], ACT.Sqrt, bias=eps_col(1)).then_inc(ln_sd, 1)
                b = filled(act, ("ln", ln, 0))
                release(nc.scalar.activation(RN[:, 0:ROWS], b[:, 0:ROWS], ACT.Copy), ("ln", ln, 0))

                def affine(b4):
                    if ln and b4 == 3:
                        act.wait_ge(last_centred, 1)
                    else:
                        act.wait_ge(xn_ready, 4 * ln + b4 + 1)
                    for k in range(4 * b4, 4 * b4 + 4):
                        y = nc.scalar.activation(tile(xT, k), tile(xT, k), ACT.Identity, scale=vec[:, scale_at + k:scale_at + k + 1],
                                                 bias=vec[:, bias_at + k:bias_at + k + 1])
                    y.then_inc(x1_ready, 1)
                return affine

            affine = normalise(0, V_G1, V_B1)
            for b4 in range(4):
                act.wait_ge(xn_ready, b4 + 1)
                if b4:
                    act.wait_ge(h2_ready, b4)
                for t in range(4):
                    s, c = (SC2 + 4 * b4 + t) * MODS, (SH2 + 4 * b4 + t) * MODS
                    y = nc.scalar.activation(tile(H2, t, 0, SEQ), tile(xT, 4 * b4 + t, 0, SEQ), ACT.Identity,
                                             scale=modT[:, s:s + 1], bias=modT[:, c:c + 1])
                y.then_inc(h2_prompt, 1)
                act.wait_ge(h2_prompt, b4 + 1)
                act.wait_ge(h2_32, b4 + 1)
                nc.scalar.activation(tiles(hH, 4 * b4, 4), tiles(H2, 0, 4), ACT.Copy).then_inc(h2H, 1)
                affine(b4)

            def up_rows(G, job, it, s_last, td, halves=2):
                banks = [0, 1, 2, 3] if halves == 2 else [0, 2]
                act.wait_ge(conv_ready, G * 2 + 2)
                act.wait_ge(tails_ready, G + 1)
                act.wait_ge(pads_set, 1)
                for n, t in enumerate(banks):
                    if n < len(banks) - 1:
                        act.wait_ge(tile_done, td + (n + 1))
                    else:
                        act.wait_ge(used, s_last + 1)
                    o = t * UW
                    nc.scalar.activation(U[:, o + 2:o + 2 + SEQ], ps[:, t, 0:SEQ], ACT.Copy)
                    release(nc.scalar.activation(spread(U[:, o + SEQ + 4:o + SEQ + 5], [TOK + 2, NSEQ], [1, TOK]),
                                                 ps[:, t, SEQ:ROWS].rearrange("p (n t) -> p n t", t=TOK), ACT.Copy), (job, t))

            def up_silu(G, gg, halves=2):
                act.wait_ge(conv_ready, G * 2 + 3)
                w = halves * CW
                nc.scalar.activation(SA[:, 0:w], CV[:, 0:w], ACT.Silu).then_inc(silu_ready, 1)
                act.wait_ge(ff32_ready, G + 1)
                nc.scalar.activation(tiles(ffH, gg * 2, halves), tiles(Ff, 0, halves), ACT.Copy).then_inc(ffH_ready, 1)

            for ph in range(3):
                s0, td, G0 = S_UP[ph], TD_UP[ph], GROUPS_BEFORE[ph]
                if ph == 0:
                    with act.Fori(0, 2) as u:
                        for i in range(1, 17):
                            half = i // 8 - 1
                            if i == 16:
                                ada_copy(u + 7, u * 16 + (A_UP + 16), turned=u + JOBS[("turn up",)][1])
                            if i % 8 == 0:
                                up_rows(u * 2 + half, ("up", 0, "ab"[half]), u, u * 16 + (s0 + i - 1), u * 6 + (td + 3 * half))
                            hi_ahead(u * 16 + s0, u * 4 + s0 // 4, i)
                            if i % 8 == 0:
                                up_silu(u * 2 + half, u * 2 + half)
                    s1, count, G1st, job, td = s0 + 32, 4, 4, ("up", 0, "c"), td + 12
                else:
                    s1, count, G1st, job = s0, UP_GROUPS[ph], G0, ("up", ph)
                with act.Fori(0, count) as g:
                    for i in range(1, 9):
                        if i == 8:
                            up_rows(g + G1st, job, g, g * 8 + (s1 + 7), g * 3 + td)
                        hi_ahead(g * 8 + s1, g * 2 + s1 // 4, i)
                        if i == 8:
                            up_silu(g + G1st, g + (G1st - G0))
                if ph == 2:
                    for i in range(1, 9):
                        s = S_UP[2] + 40 + i + AHEAD
                        if i == 8:
                            up_rows(G0 + 5, ("up tail",), 0, S_UP[2] + 47, td + 15, halves=1)
                        hi(s, s // 4, s % 4, slab_columns(s))
                        if i == 8:
                            up_silu(G0 + 5, 5, halves=1)
                if ph < 2:
                    with act.Fori(0, 4) as g:
                        for i in range(1, 9):
                            hi_ahead(g * 8 + S_DN[ph], g * 2 + S_DN[ph] // 4, i)
                else:
                    for g in range(4):
                        for j in range(6):
                            q = 6 * g + j
                            if 0 < q < 24 - AHEAD:
                                s = S_DN[2] + q + AHEAD
                                hi(s, s // 4, s % 4, slab_columns(s))
                            if g and j == 0:
                                copy_sum(g - 1, 1)
            affine = normalise(1, V_G2, V_B2)
            for b4 in range(4):
                affine(b4)
                act.wait_ge(x1_ready, 4 + b4 + 1)
                act.dma_start(io["yT"][:, b4 * 4 * ROWS:(b4 + 1) * 4 * ROWS], xT[:, b4 * 4 * ROWS:(b4 + 1) * 4 * ROWS]).then_inc(stored, 16)
            act.wait_ge(stored, 16 * 4)



        @block.vector
        def _(dve):
            steps = Steps(dve, dve_step)
            vec_tt, vec_ts, vec_stt = nc.vector.tensor_tensor, nc.vector.tensor_scalar, nc.vector.scalar_tensor_tensor

            def lo(s, slot, cols=SLAB):
                dve.wait_ge(hi_done, s + 1)
                o = slot * SLAB
                vec_tt(wL[:, o:o + cols], raw[:, o:o + cols], wH[:, o:o + cols].bitcast(F32), ALU.subtract).then_inc(split_done, 1)

            def mod_finish(job, bases, it=0, gate=False):
                def entries(t, base_tile, n, at=0):
                    if isinstance(base_tile, int):
                        return t[:, at + base_tile * n:at + (base_tile + 4) * n]
                    return t[:, bass.ds(base_tile * n + at, 4 * n)]
                b = filled(dve, job, it)
                for q, base_tile in enumerate(bases):
                    src = spread(b[:, 64 * (q % 2) + 256 * (q // 2):64 * (q % 2) + 256 * (q // 2) + 1], [32, 2], [P, 2], [1, MODS])
                    ins = vec_tt(spread(entries(modT, base_tile, MODS), [2 * MODS, 2], [MODS, 2], [1, MODS]), src,
                                 spread(entries(vec, base_tile, 1, V_ADA), [2, 2], [1, 2], [0, MODS]), ALU.add)
                release(ins, job)
                released(dve, job, it)
                if gate:
                    for base_tile in bases:
                        v = entries(modT, base_tile, MODS)
                        ins = vec_ts(v, v, 1.0 / ALPHA, None, ALU.mult)
                    steps.link(ins)

            def modulate(dst, src, scale_tile, shift_tile, k, done):
                dp, dd = tiles(dst, 0, 4, 0, SEQ), by_seq(tiles(dst, 0, 4, SEQ, ROWS), 4)
                scale, shift = mods(scale_tile, 4), mods(shift_tile, 4)
                vec_tt(dp, tiles(src, k, 4, 0, SEQ), scale[0], ALU.mult)
                steps.link(vec_tt(dd, by_seq(tiles(src, k, 4, SEQ, ROWS), 4), scale[1], ALU.mult))
                vec_tt(dp, dp, shift[0], ALU.add)
                vec_tt(dd, dd, shift[1], ALU.add).then_inc(done, 1)

            def h_lo(kg):
                dve.wait_ge(hH_ready, kg + 1)
                vec_tt(tiles(hL, kg * 4, 4), tiles(H32, 0, 4), tiles(hH, kg * 4, 4).bitcast(F32), ALU.subtract).then_inc(h_ready, 1)

            for bank in range(5):
                dve.sem_inc(bank_free[bank], 1)
            dve.sem_inc(conv_ready, 2)
            nc.vector.memset(ones[:, :], 1.0)
            nc.vector.memset(small[:, :], 1.0)
            steps.link(nc.vector.memset(cw[:, :], 0.0))
            nc.vector.memset(small[:, 140:141], EPS)
            nc.vector.memset(small[:, 141:142], EPS / ALPHA ** 2)
            dve.wait_ge(small_in, 16 * 2)
            for scale_at in (V_ADA + 16, V_ADA + SC2):
                vec_ts(vec[:, scale_at:scale_at + 16], vec[:, scale_at:scale_at + 16], 1.0, None, ALU.add)
            b = filled(dve, "bias")
            nc.vector.tensor_copy(bvec[:, 0:REL_N], spread(b[0:HEADS, REL_N - 1:REL_N], [-1, REL_N]))
            release(nc.vector.tensor_copy(bvec[:, REL_N:2 * REL_N], b[0:HEADS, 0:REL_N]), "bias")
            released(dve, "bias")
            for s in range(AHEAD):
                lo(s, s)
            mod_finish(("turn", 0), (0, 16))
            dve.wait_ge(x_in, 16)
            modulate(H32, xT, 16, 0, 0, h32_ready)
            h_lo(0)

            dve.wait_ge(proj_zeroed, 1)
            dve.wait_ge(x_rest_in, 16)

            def w_in_quarter(kg, it, loop):
                for i in range(1, IN_STEPS + 1):
                    if i % 2 == 0:
                        lo(kg * IN_STEPS + (i + AHEAD), (i + AHEAD) % RING)
                    if i == ADA_STEPS + 2 and loop:
                        h_lo(kg + 1)
                    if i % 2:
                        g = i // 2
                        for t in range(4):
                            if t < 3:
                                dve.wait_ge(tile_done, kg * 30 + (TD_IN + 3 * g + t + 1))
                            else:
                                dve.wait_ge(used, kg * IN_STEPS + (i + 1))
                            k = 4 * g + t
                            release(vec_tt(tile(proj, k), ps[:, k % 5, 0:ROWS], tile(proj, k), ALU.add), ("in", loop, k))
                        lo(kg * IN_STEPS + (i + AHEAD), (i + AHEAD) % RING)
                    if i == ADA_STEPS:
                        if loop:
                            mod_finish(("turn in", loop), (kg * 4 + 4, kg * 4 + 20, kg * 8 + SH2, kg * 8 + (SH2 + 4)), it)
                            modulate(H32, xT, kg * 4 + 20, kg * 4 + 4, kg * 4 + 4, h32_ready)
                        else:
                            mod_finish(("turn in", loop), (SC2 + 8, SC2 + 12), it)

            lo(AHEAD, AHEAD)
            with dve.Fori(0, 3) as kg:
                steps.enter(kg, 1)
                w_in_quarter(kg, kg, True)
                steps.leave(3)
            w_in_quarter(3, 0, False)
            nc.vector.memset(small[:, 159:160], 0.0).then_inc(proj_ready, 1)
            dve.wait_ge(gate_in, 32)
            w = wsT[:, :].rearrange("p (g t) -> p g t", g=HEADS)
            vec_tt(w, w, spread(cst[:, C_TRI:C_TRI + P], [0, HEADS], [1, P]), ALU.mult)
            w = bd[:, :].rearrange("p (g t) -> p g t", g=HEADS)
            vec_tt(w, w, spread(cst[0:SAMP, C_BD:C_BD + SAMP], [0, HEADS], [1, SAMP]), ALU.mult)

            dve.wait_ge(bvec_stored, 16)
            for hg in range(2):
                b = filled(dve, ("v", 2, hg))
                release(nc.vector.tensor_copy(Vn[:, hg * 512:(hg + 1) * 512], b[0:SAMP, :]), ("v", 2, hg))
            for r in range(3):
                n = P if r < 2 else SAMP
                for hg in range(2):
                    b = filled(dve, ("va", r, hg))
                    ins = nc.vector.bn_stats(small[0:n, 12 * r + 6 * hg:12 * r + 6 * hg + 6], b[0:n, :])
                steps.link(ins)
                nc.vector.bn_aggr(small[0:n, 36 + 2 * r:38 + 2 * r], small[0:n, 12 * r:12 * r + 12]).then_inc(var_ready, 1)
            dve.wait_ge(va_sd, 1)
            steps.link(nc.vector.reciprocal(small[:, 42:45], small[:, 42:45]))
            dve.wait_ge(sgu_in, 16 * 3)
            for r in range(3):
                n = P if r < 2 else SAMP
                dst = VA[:, r * 1024:(r + 1) * 1024] if r < 2 else VAs[:, :]
                for hg in range(2):
                    b = filled(dve, ("va", r, hg))
                    ins = vec_ts(dst[:, hg * 512:(hg + 1) * 512], b[0:n, :], small[0:n, 36 + 2 * r:37 + 2 * r],
                                 small[0:n, 42 + r:43 + r], ALU.subtract, ALU.mult)
                    release(ins, ("va", r, hg))
                released(dve, ("va", r, 1))
                steps.link(vec_tt(dst, dst, SG[0:n, :], ALU.mult))
                vec_tt(dst, dst, SH[0:n, :], ALU.add).then_inc(va_ready, 1)

            dve.wait_ge(gelu_ready, 2)
            for c in range(2):
                for gg in range(2):
                    b = filled(dve, ("gate", c, gg))
                    release(vec_tt(Tm[:, gg * 512:(gg + 1) * 512], b, BS[:, gg * 512:(gg + 1) * 512], ALU.add), ("gate", c, gg))
                for gg in range(2):
                    released(dve, ("gate", c, gg))
                    u = tiles(proj, 24 + 4 * gg, 4, c * P, (c + 1) * P)
                    ins = vec_tt(u, u, Tm[:, gg * 512:(gg + 1) * 512].rearrange("p (g t) -> p g t", g=4), ALU.mult)
                steps.link(ins)
            b = filled(dve, "gate decode")
            release(vec_tt(spread(Tm[:, 0:1], [SAMP, HEADS], [TOK, NSEQ], [1, TOK]), spread(b[:, 0:1], [SAMP, HEADS], [TOK, NSEQ], [1, TOK]),
                           spread(BS[:, 0:1], [P, HEADS], [0, NSEQ], [1, TOK]), ALU.add), "gate decode")
            released(dve, "gate decode")
            u = tiles(proj, 24, 8, SEQ, ROWS)
            vec_tt(u, u, Tm[:, 0:256].rearrange("p (g t) -> p g t", g=HEADS), ALU.mult).then_inc(gm_ready, 1)

            dve.wait_ge(table_in, TABLES * 16)
            sbn = spread(SBi[:, PAST:PAST + 1], [ROWS, 2], [TOK, NSEQ], [1, TOK])
            steps.link(vec_tt(sbn, spread(E4[:, 0:1], [TOK, 2], [0, NSEQ], [1, TOK]),
                              spread(cst[:, C_MP:C_MP + 1], [0, 2], [TOK, NSEQ], [1, TOK]), ALU.mult))

            def own_queries(n):
                if n >= 2:
                    dve.wait_ge(kv_used, n - 1)
                q = Qm[:, (n % 2) * 256:(n % 2 + 1) * 256].rearrange("p (h c) -> p h c", h=HEADS)
                vec_tt(q, tiles(proj, 0, 8, SEQ, ROWS), spread(cst[:, C_M32 + n * SAMP:C_M32 + n * SAMP + 1], [0, HEADS], [1, SAMP]),
                       ALU.mult).then_inc(qm_ready, 1)

            own_queries(0)
            own_queries(1)
            steps.link(vec_tt(sbn, sbn, spread(cst[:, C_MN:C_MN + 1], [0, 2], [TOK, NSEQ], [1, TOK]), ALU.add))
            b = filled(dve, "S new")
            release(vec_stt(spread(Ls[:, PAST:PAST + 1], [ROWS, 2], [1, SAMP]), spread(b[:, 0:1], [SAMP, 2], [1, SAMP]), SCALE,
                            spread(SBi[:, PAST:PAST + 1], [ROWS, 2], [1, SAMP]), ALU.mult, ALU.add), "S new")

            mod_finish(("turn", 4), (G1, G1 + 4), gate=True)

            def all_mods(k):
                return modT[:, k * MODS:(k + KT) * MODS].rearrange("p (k c) -> p k c", k=KT)

            def columns(at):
                return spread(vec[:, at:at + KT], [1, KT], [0, MODS])

            def fold_norm():
                steps.link(vec_tt(all_mods(0), all_mods(SC2), columns(V_B1), ALU.mult))
                vec_tt(all_mods(SH2), all_mods(SH2), all_mods(0), ALU.add)
                steps.link(vec_tt(all_mods(SC2), all_mods(SC2), columns(V_G1), ALU.mult))

            def invert_root(a):
                released(dve, ("sum a", "sum b")[a])
                rr = RR[:, a * ROWS:(a + 1) * ROWS]
                steps.link(nc.vector.reciprocal(rr, rr))

            def norm_rows(a, half):
                m = tiles(proj, (24, 0)[a] + 4 * half, 4)
                vec_tt(m, m, spread(RR[:, a * ROWS:a * ROWS + 1], [0, 4], [1, ROWS]), ALU.mult).then_inc(m_ready, 1)

            def mix_lo_at(k):
                dve.wait_ge(mH_ready, k + 1)
                vec_stt(mix_lo(k), mixed(k), vec[:, V_NA + k:V_NA + k + 1], mix_hi(k).bitcast(F32), ALU.mult,
                        ALU.subtract).then_inc(m_split, 1)

            for h in range(HEADS + 1):
                if h < HEADS:
                    o, m = (h % 2) * 384, 50 + 2 * (h % 2)
                    if h >= 2:
                        dve.wait_ge(exp_ready, h - 1)
                    b = filled(dve, ("S", h))
                    vec_stt(Lp[:, o:o + P], b[:, 0:P], SCALE, spread(TB[:, h * 256 + P - 1:h * 256 + P], [-1, P]), ALU.mult, ALU.add)
                    release(vec_stt(Lp[:, o + P:o + 384], b[:, P:384], SCALE, spread(TB[:, h * 256 + 255:h * 256 + 256], [-1, 256]), ALU.mult, ALU.add), ("S", h))
                    released(dve, ("S", h))
                    nc.vector.tensor_reduce(small[:, m:m + 1], Lp[:, o:o + P], AX.X, ALU.max, negate=True)
                    nc.vector.tensor_reduce(small[:, m + 1:m + 2], Lp[:, o + P:o + 384], AX.X, ALU.max, negate=True).then_inc(logit_ready, 1)
                if h:
                    o, m = ((h - 1) % 2) * 384, 54 + 2 * ((h - 1) % 2)
                    dve.wait_ge(exp_ready, h)
                    steps.link(nc.vector.reciprocal(small[:, m:m + 2], small[:, m:m + 2]))
                    vec_ts(Pp[:, o:o + P], Pp[:, o:o + P], small[:, m:m + 1], None, ALU.mult)
                    vec_ts(Pp[:, o + P:o + 384], Pp[:, o + P:o + 384], small[:, m + 1:m + 2], None, ALU.mult).then_inc(prob_ready, 1)
                    if h + 1 < NSEQ:
                        own_queries(h + 1)
                if h == 1:
                    fold_norm()
                if h == 2:
                    invert_root(0)
                    norm_rows(0, 0)
                if h == 3:
                    norm_rows(0, 1)
                if h >= 5:
                    mix_lo_at(2 * h - 10)
                    mix_lo_at(2 * h - 9)

            dve.wait_ge(kv_used, NSEQ)
            for hh in range(2):
                release(vec_stt(Ls[:, hh * ROWS:hh * ROWS + PAST], ps[:, 6 + hh, 0:PAST], SCALE, SBi[:, hh * ROWS:hh * ROWS + PAST],
                                ALU.mult, ALU.add), f"S past {hh}")
            released(dve, "S past 1")
            nc.vector.tensor_reduce(small[:, 58:60], Ls[:, :].rearrange("p (a c) -> p a c", a=2), AX.X, ALU.max, negate=True).then_inc(s_logit, 1)
            dve.wait_ge(s_exp, 1)
            steps.link(nc.vector.reciprocal(small[:, 60:62], small[:, 60:62]))
            for hh in range(2):
                ins = vec_ts(Ls[:, hh * ROWS:(hh + 1) * ROWS], Ls[:, hh * ROWS:(hh + 1) * ROWS], small[:, 60 + hh:61 + hh], None, ALU.mult)
            ins.then_inc(s_prob, 1)

            def tile_filled(t, td, s_last):
                if t < 3:
                    dve.wait_ge(tile_done, td + (t + 1))
                else:
                    dve.wait_ge(used, s_last + 1)

            def out_step(n):
                lo(S_OUT + n + AHEAD, (n + AHEAD) % RING)

            def accumulate_out(g):
                for t, bank in enumerate(OUT_BANKS):
                    tile_filled(t, TD_OUT + 3 * g, S_OUT + 4 * g + 3)
                    n, x = G1 + 4 * g + t, tile(xT, 4 * g + t, 0, SEQ)
                    vec_tt(by_seq(tiles(S4, t, 1, SEQ, ROWS), 1), by_seq(ps[:, bank:bank + 1, SEQ:ROWS], 1), mods(n, 1)[1], ALU.mult)
                    release(vec_stt(x, ps[:, bank, 0:SEQ], modT[:, n * MODS:n * MODS + 1], x, ALU.mult, ALU.add), ("out a", g, t))
                released(dve, ("out a", g, 3))
                x = tiles(xT, 4 * g, 4, SEQ, ROWS)
                steps.link(vec_tt(x, x, tiles(S4, 0, 4, SEQ, ROWS), ALU.add))

            out_step(1)
            out_step(2)
            b = filled(dve, "s PN")
            release(nc.vector.tensor_copy(PN[:, :], b[0:SAMP, 0:256]), "s PN")
            released(dve, "s PT")

            def own_probabilities(n):
                if n >= 2:
                    dve.wait_ge(kv_used, NSEQ + n - 1)
                vec_tt(PTm[:, (n % 2) * 512:(n % 2 + 1) * 512].rearrange("p (a c) -> p a c", a=16),
                       PTs[:, :].rearrange("p (a c) -> p a c", a=16),
                       spread(cst[:, C_M32 + n * SAMP:C_M32 + n * SAMP + 1], [0, 16], [1, SAMP]), ALU.mult).then_inc(ptm_ready, 1)

            own_probabilities(0)
            for n in range(NSEQ):
                if n + 1 < NSEQ:
                    own_probabilities(n + 1)
                if n in (2, 6):
                    accumulate_out(n // 4)
                if n:
                    out_step(2 + n)
            for hh in range(2):
                b = filled(dve, f"O {hh}")
                release(nc.vector.tensor_copy(OS[:, hh * P:(hh + 1) * P], b[:, 0:P]), f"O {hh}")
            out_step(10)
            mod_finish(("turn", 5), (G1 + 8, G1 + 12), gate=True)
            out_step(11)
            accumulate_out(2)
            out_step(12)
            out_step(13)
            invert_root(1)
            norm_rows(1, 0)
            norm_rows(1, 1)
            for k in range(8, 12):
                mix_lo_at(k)
            out_step(14)
            for k in range(12, 16):
                mix_lo_at(k)
            out_step(15)
            accumulate_out(3)
            out_step(16)

            def residual(g, ln, job, gate_tile, td, s_last):
                if ln or g:
                    dve.wait_ge(s4_copied, 4 * ln + g)
                for t in range(4):
                    tile_filled(t, td, s_last)
                    n = gate_tile + 4 * g + t
                    vec_tt(by_seq(tiles(S4, t, 1, SEQ, ROWS), 1), by_seq(ps[:, t:t + 1, SEQ:ROWS], 1), mods(n, 1)[1], ALU.mult)
                    ins = vec_stt(tile(S4, t, 0, SEQ), ps[:, t, 0:SEQ], modT[:, n * MODS:n * MODS + 1], tile(xT, 4 * g + t, 0, SEQ),
                                  ALU.mult, ALU.add)
                    release(ins, job(t))
                released(dve, job(3))
                vec_tt(tiles(S4, 0, 4, SEQ, ROWS), tiles(S4, 0, 4, SEQ, ROWS), tiles(xT, 4 * g, 4, SEQ, ROWS), ALU.add).then_inc(s4_ready, 1)

            def row_statistics(g, ln):
                for r in range(3):
                    n, job = P if r < 2 else SAMP, ("rows", ln, g, r)
                    b = filled(dve, job)
                    release(nc.vector.bn_stats(small[0:n, 50 + 24 * r + 6 * g:56 + 24 * r + 6 * g], b[0:n, :]), job)

            def normalise(ln):
                row_statistics(3, ln)
                released(dve, ("rows", ln, 3, 2))
                for r in range(3):
                    n = P if r < 2 else SAMP
                    ins = nc.vector.bn_aggr(small[0:n, 134 + 2 * r:136 + 2 * r], small[0:n, 50 + 24 * r:74 + 24 * r])
                steps.link(ins)
                nc.vector.tensor_copy(small[:, 126:129], spread(small[:, 135:136], [2, 3])).then_inc(ln_var, 1)
                dve.wait_ge(ln_sd, ln + 1)
                steps.link(nc.vector.reciprocal(small[:, 142:145], small[:, 130:133]))
                steps.link(vec_stt(small[:, 145:148], spread(small[:, 134:135], [2, 3]), -1.0, small[:, 142:145], ALU.mult, ALU.mult))
                for r in range(3):
                    n = P if r < 2 else SAMP
                    for j in range(2):
                        ins = vec_ts(DG[0:n, (2 * r + j) * P:(2 * r + j) * P + n], ident[0:n, 0:n],
                                     small[0:n, 142 + 3 * j + r:143 + 3 * j + r], None, ALU.mult)
                ins.then_inc(diag_ready, 1)
                b = filled(dve, ("ln", ln, 1))
                dve.wait_ge(s4_copied, 4 * ln + 4)
                release(nc.vector.tensor_copy(RN[:, ROWS:2 * ROWS], b[:, 0:ROWS]), ("ln", ln, 1))
                released(dve, ("ln", ln, 0))
                released(dve, ("ln", ln, 1))

            def centre(b4, ln):
                x = tiles(xT, 4 * b4, 4)
                steps.link(vec_tt(x, x, spread(RN[:, 0:1], [0, 4], [1, ROWS]), ALU.mult))
                vec_tt(x, x, spread(RN[:, ROWS:ROWS + 1], [0, 4], [1, ROWS]), ALU.add).then_inc(xn_ready, 1)

            for g in range(4):
                for j in range(1, 5):
                    if j == 4:
                        residual(g, 0, lambda t: ("out", g, t), G1, TD_OUT + 12 + 3 * g, S_OUT + 19 + 4 * g)
                    out_step(16 + 4 * g + j)
                    if g and j == 2:
                        row_statistics(g - 1, 0)
            normalise(0)
            centre(0, 0)
            for b4 in range(4):
                samp, x = by_seq(tiles(H2, 0, 4, SEQ, ROWS), 4), by_seq(tiles(xT, 4 * b4, 4, SEQ, ROWS), 4)
                dve.wait_ge(xn_ready, b4 + 1)
                if b4:
                    dve.wait_ge(h2_ready, b4)
                steps.link(vec_tt(samp, x, mods(SC2 + 4 * b4, 4)[1], ALU.mult))
                vec_tt(samp, samp, mods(SH2 + 4 * b4, 4)[1], ALU.add).then_inc(h2_32, 1)
                if b4 < 3:
                    centre(b4 + 1, 0)
                dve.wait_ge(h2H, b4 + 1)
                vec_tt(tiles(hL, 4 * b4, 4), tiles(H2, 0, 4), tiles(hH, 4 * b4, 4).bitcast(F32), ALU.subtract).then_inc(h2_ready, 1)

            def convolve(G, job, it, halves):
                dve.wait_ge(past_ready, G + 1)
                for pair in range(2):
                    both = [2 * pair, 2 * pair + 1][:halves]
                    for t in both:
                        released(dve, (job, t), it)
                    cv, u = lambda t: CV[:, t * CW:(t + 1) * CW], lambda t, d: U[:, t * UW + d:t * UW + d + CW]
                    for t in both:
                        ins = vec_ts(cv(t), u(t, 0), cw[:, 4 * t:4 * t + 1], cw[:, 4 * t + 3:4 * t + 4], ALU.mult, ALU.add)
                    steps.link(ins)
                    for t in both:
                        ins = vec_stt(cv(t), u(t, 1), cw[:, 4 * t + 1:4 * t + 2], cv(t), ALU.mult, ALU.add)
                    steps.link(ins)
                    for t in both:
                        ins = vec_stt(cv(t), u(t, 2), cw[:, 4 * t + 2:4 * t + 3], cv(t), ALU.mult, ALU.add)
                    ins.then_inc(conv_ready, 1)

            def gated(G, gg, halves):
                dve.wait_ge(silu_ready, G + 1)
                dve.wait_ge(conv_ready, G * 2 + 4)
                a, v = SA[:, 0:halves * CW].rearrange("p (k c) -> p k c", k=halves), CV[:, 2 * CW:(2 + halves) * CW].rearrange("p (k c) -> p k c", k=halves)
                rows = lambda x: spread(x[:, :, SEQ + 2:SEQ + 3], [CW, halves], [TOK + 2, NSEQ], [1, TOK])
                vec_tt(tiles(Ff, 0, halves, 0, SEQ), a[:, :, 0:SEQ], v[:, :, 0:SEQ], ALU.mult)
                vec_tt(by_seq(tiles(Ff, 0, halves, SEQ, ROWS), halves), rows(a), rows(v), ALU.mult).then_inc(ff32_ready, 1)
                dve.wait_ge(ffH_ready, G + 1)
                vec_tt(tiles(ffL, gg * 2, halves), tiles(Ff, 0, halves), tiles(ffH, gg * 2, halves).bitcast(F32),
                       ALU.subtract).then_inc(ff_ready, 1)

            def accumulate(g, ph, td, s_last):
                S4d = tiles(S4, 0, 4, SEQ, ROWS)
                for t in range(4):
                    tile_filled(t, td, s_last)
                    if t == 0:
                        dve.wait_ge(x1_ready, 4)
                        nc.vector.tensor_copy(small[:, 148:152], spread(modT[:, bass.ds(g * (4 * MODS) + G2 * MODS, 1)], [MODS, 4])).then_inc(dve_step, 1)
                        steps.n += 1
                    gates = spread(modT[:, bass.ds(g * (4 * MODS) + ((G2 + t) * MODS + 1), 1)], [MODS, 1], [1, NSEQ], [0, TOK])
                    vec_tt(by_seq(S4d[:, t:t + 1, :], 1), by_seq(ps[:, t:t + 1, SEQ:ROWS], 1), gates, ALU.mult)
                    if t == 0:
                        dve.wait_ge(dve_step, g + steps.n)
                    x = xT[:, bass.ds(g * (4 * ROWS) + t * ROWS, SEQ)]
                    release(vec_stt(x, ps[:, t, 0:SEQ], small[:, 148 + t:149 + t], x, ALU.mult, ALU.add), ("down", ph, t))
                released(dve, ("down", ph, 3), g)
                x = tiles(xT, g * 4, 4, SEQ, ROWS)
                vec_tt(x, x, S4d, ALU.add)

            for ph in range(3):
                s0, G0 = S_UP[ph], GROUPS_BEFORE[ph]
                if ph == 0:
                    with dve.Fori(0, 2) as u:
                        steps.enter(u, 9)
                        for i in range(1, 17):
                            if i % 8 == 0:
                                convolve(u * 2 + i // 8 - 1, ("up", 0, "ab"[i // 8 - 1]), u, 2)
                            lo(u * 16 + (s0 + i + AHEAD), (i + AHEAD) % RING)
                            if i % 8 == 0:
                                gated(u * 2 + i // 8 - 1, u * 2 + i // 8 - 1, 2)
                        mod_finish(("turn up",), (u * 8 + G2, u * 8 + (G2 + 4)), u, gate=True)
                        steps.leave(2)
                    loops = [(4, s0 + 32, 4, ("up", 0, "c"))]
                else:
                    loops = [(UP_GROUPS[ph], s0, G0, ("up", ph))]
                for count, s1, G1st, job in loops:
                    with dve.Fori(0, count) as g:
                        steps.enter(g, 4)
                        for i in range(1, 9):
                            if i == 8:
                                convolve(g + G1st, job, g, 2)
                            lo(g * 8 + (s1 + i + AHEAD), (i + AHEAD) % RING)
                            if i == 8:
                                gated(g + G1st, g + (G1st - G0), 2)
                        steps.leave(count)
                if ph == 2:
                    for i in range(1, 9):
                        s = S_UP[2] + 40 + i + AHEAD
                        if i == 8:
                            convolve(G0 + 5, ("up tail",), 0, 1)
                        lo(s, s % RING, slab_columns(s))
                        if i == 8:
                            gated(G0 + 5, 5, 1)
                if ph < 2:
                    with dve.Fori(0, 4) as g:
                        steps.enter(g, 1)
                        for i in range(1, 9):
                            if i == 8:
                                accumulate(g, ph, g * 3 + TD_DN[ph], g * 8 + (S_DN[ph] + 7))
                            lo(g * 8 + (S_DN[ph] + i + AHEAD), (i + AHEAD) % RING)
                        steps.leave(4)
                else:
                    for g in range(4):
                        for j in range(6):
                            q = 6 * g + j
                            s = S_DN[2] + q + AHEAD
                            if j == 5:
                                residual(g, 1, lambda t: ("down", 2, g, t), G2, TD_DN[2] + 3 * g, S_DN[2] + 6 * g + 5)
                            if 0 < q < 24 - AHEAD:
                                lo(s, s % RING, slab_columns(s))
                            if g and j == 3:
                                row_statistics(g - 1, 1)
            normalise(1)
            for b4 in range(3):
                centre(b4, 1)

        @block.gpsimd
        def _(pool):
            copy = nc.gpsimd.tensor_copy
            pool.sem_inc(tails_ready, 1)
            pool.dma_start(cst[:, :], io["cst"][:, :]).then_inc(small_in, 16)
            pool.dma_start(vec[:, :], io["vec"][:, :]).then_inc(small_in, 16)
            pool.dma_start(hot[:, :], io["hot"][:, :]).then_inc(bias_in, 16)
            pool.dma_start(rbias[:, :], io["rbias"][:, :]).then_inc(bias_in, 16)
            pool.dma_start(pages[:, :], io["pages"][:, :]).then_inc(pages_in, 16)
            nc.gpsimd.memset(proj[:, :], 0.0).then_inc(proj_zeroed, 1)
            released(pool, "bias")
            pool.dma_start(bias_rows[:, :].rearrange("(a h) c -> h a c", a=2), bvec[:, :].rearrange("h (a c) -> h a c", a=2)).then_inc(bvec_stored, 16)

            pool.wait_ge(h32_ready, 2)
            pool.dma_start(wsT[:, :], io["wsT"][:, :]).then_inc(gate_in, 16)
            pool.dma_start(bd[:, :], io["bd"][:, :]).then_inc(gate_in, 16)

            def load_rows(at, name):
                pool.dma_start(at[:, :], bass.AP(io[name].tensor, 0, [[0, P], [1, 1024]])).then_inc(sgu_in, 16)

            load_rows(SG, "sgu_g")
            load_rows(SH, "sgu_b")

            pool.wait_ge(proj_ready, 1)
            load_rows(BS, "b_s")
            pool.wait_ge(pages_in, 16)

            def load_kv(idx):
                n, name = idx % NSEQ, "keys" if idx < NSEQ else "values"
                if idx >= 2:
                    pool.wait_ge(kv_used, idx - 1)
                for pg in range(PAGES):
                    page = pool.value_load(pages[0:1, n * PAGES + pg:n * PAGES + pg + 1], min_val=0, max_val=n_phys - 1)
                    o = (idx % 2) * 2048 + pg * 1024
                    pool.dma_start(KV[:, o:o + 1024], io[name][bass.ds(page, 1), :, :].rearrange("a p c -> (a p) c")).then_inc(kv_in[idx % 2], 16)

            pool.dma_start(io["kvT"][:, :], proj[:, 8 * ROWS:24 * ROWS]).then_inc(kv_stored, 16)
            pool.wait_ge(bvec_stored, 16)
            rows = bias_rows.tensor
            pool.dma_start(TB[:, :].rearrange("p (h c) -> p h c", h=HEADS),
                           bass.AP(rows, 0, [[1, P], [REL_N, HEADS], [1, 256]])).then_inc(table_in, 16)
            for hh in range(2):
                for t in range(TOK):
                    pool.dma_start(SBi[t:P:TOK, hh * ROWS:hh * ROWS + PAST],
                                   bass.AP(rows, HEADS * REL_N + 4 * hh * REL_N + TOK - 1 - t, [[REL_N, 4], [0, NSEQ], [1, PAST]])).then_inc(table_in, 16)
                    pool.dma_start(E4[t:P:TOK, hh * TOK:(hh + 1) * TOK],
                                   bass.AP(rows, HEADS * REL_N + 4 * hh * REL_N + REL_MAX - t, [[REL_N, 4], [0, NSEQ], [1, TOK]])).then_inc(table_in, 16)
            load_kv(0)
            load_kv(1)
            pool.wait_ge(va_ready, 3)
            pool.dma_start(past[:, :], io["past"][:, :]).then_inc(past_in, 16)
            pool.dma_start(io["va"][:, :], VAs[:, :]).then_inc(va_stored, 16)
            for idx in range(2, 2 * NSEQ):
                load_kv(idx)

            pool.wait_ge(past_in, 16)
            pool.wait_ge(m_split, 9)
            nc.gpsimd.memset(spread(U[:, 0:1], [UW, 4], [1, 2]), 0.0).then_inc(pads_set, 1)

            def flat(t, k, step, n):
                return t[:, k * step:(k + n) * step] if isinstance(k, int) else t[:, bass.ds(k * step, n * step)]

            def group(G, job, it, halves=2):
                pool.wait_ge(conv_ready, G * 2 + 2)
                for pair, first in ((0, G * 2), (1, G * 2 + FT)):
                    copy(spread(U[:, 2 * pair * UW + SEQ + 2:2 * pair * UW + SEQ + 3], [UW, halves], [TOK + 2, NSEQ], [1, 2]),
                         spread(flat(past, first, 16, halves), [16, halves], [2, NSEQ], [1, 2]))
                    ins = copy(cw[:, 8 * pair:8 * pair + 4 * halves], flat(taps, first, 4, halves))
                ins.then_inc(past_ready, 1)
                for pair, first in ((0, G * 2), (1, G * 2 + FT)):
                    for t in range(2 * pair, 2 * pair + halves):
                        released(pool, (job, t), it)
                    e = flat(E, first, 18, halves)
                    o = 2 * pair * UW
                    copy(spread(e, [18, halves], [1, 2]), spread(U[:, o + SEQ:o + SEQ + 1], [UW, halves], [1, 2]))
                    ins = copy(spread(e.rearrange("p (k c) -> p k c", k=halves)[:, :, 2:18], [18, halves], [2, NSEQ], [1, 2]),
                               spread(U[:, o + SEQ + 6:o + SEQ + 7], [UW, halves], [TOK + 2, NSEQ], [1, 2]))
                ins.then_inc(tails_ready, 1)

            taps = vec[:, V_CONV:V_ALL]
            with pool.Fori(0, 2) as u:
                group(u * 2, ("up", 0, "a"), u)
                group(u * 2 + 1, ("up", 0, "b"), u)
            with pool.Fori(0, 4) as g:
                group(g + 4, ("up", 0, "c"), g)
            for ph in (1, 2):
                with pool.Fori(0, UP_GROUPS[ph]) as g:
                    group(g + GROUPS_BEFORE[ph], ("up", ph), g)
            group(GROUPS_BEFORE[2] + 5, ("up tail",), 0, 1)
            pool.wait_ge(tails_ready, GROUPS_BEFORE[2] + 7)
            pool.dma_start(io["tails"][:, :], E[:, :]).then_inc(tails_stored, 16)
            pool.wait_ge(s4_copied, 8)
            released(pool, ("ln", 1, 0))
            released(pool, ("ln", 1, 1))
            x = tiles(xT, 12, 4)
            nc.gpsimd.tensor_tensor(x, x, spread(RN[:, 0:1], [0, 4], [1, ROWS]), ALU.mult).then_inc(last_scaled, 1)
            pool.wait_ge(last_scaled, 1)
            nc.gpsimd.tensor_tensor(x, x, spread(RN[:, ROWS:ROWS + 1], [0, 4], [1, ROWS]), ALU.add).then_inc(last_centred, 1)
            pool.wait_ge(tails_stored, 16)
            pool.wait_ge(kv_stored, 16)
            pool.wait_ge(va_stored, 16)


def kernel(**inputs):
    from concourse import bacc
    from concourse.bass_utils import run_bass_kernel_spmd

    a = {k: np.asarray(v) for k, v in inputs.items()}
    f = np.ascontiguousarray

    def rows_t(p, s):
        x = np.concatenate([p.reshape(SEQ, -1), s.reshape(SAMP, -1)], 0)
        return f(x.T.reshape(-1, P, ROWS).transpose(1, 0, 2).reshape(P, -1))

    w_in = a["w_in"][0].reshape(KT, P, 4 * IN_GROUPS, P)
    w_in_s = f(np.stack([w_in[4 * kg + 2 * half:4 * kg + 2 * half + 2, :, 4 * g:4 * g + 4].transpose(1, 0, 2, 3).reshape(P, -1)
                         for kg in range(4) for g in range(IN_GROUPS) for half in range(2)]))
    w_out = a["w_out"][0]
    w_up = a["w_up"][0]
    w_down = a["w_down"][0]
    tile_of = lambda k: slice(k * P, (k + 1) * P)

    def slab(w, ks, ns):
        return np.stack([w[tile_of(k)][:, np.concatenate([np.arange(n * P, (n + 1) * P) for n in ns])] for k in ks], 1).reshape(P, -1)

    w_out_s = f(np.stack([slab(w_out, (2 * j, 2 * j + 1), range(4 * g, 4 * g + 4)) for j0 in (0, 4) for g in range(4) for j in range(j0, j0 + 4)]))
    up_tiles = [[16 * ph + 2 * gg, 16 * ph + 2 * gg + 1, FT + 16 * ph + 2 * gg, FT + 16 * ph + 2 * gg + 1]
                for ph in range(3) for gg in range(UP_GROUPS[ph])]
    w_up_s = f(np.stack([slab(w_up, (2 * j, 2 * j + 1), ns) for ns in up_tiles for j in range(8)]))
    w_up_tail = f(np.stack([slab(w_up, (2 * j, 2 * j + 1), (FT - 1, 2 * FT - 1)) for j in range(8)]))
    down = [(2 * j, g) for g in range(4) for j in range(8)] + [(16 + 2 * j, g) for g in range(4) for j in range(8)] + \
           [(32 + 2 * j, g) for g in range(4) for j in range(5)]
    w_down_s = f(np.stack([slab(w_down, (k, k + 1), range(4 * g, 4 * g + 4)) for k, g in down]))
    w_down_tail = f(np.stack([slab(w_down, (FT - 1,), range(4 * g, 4 * g + 4)) for g in range(4)]))
    w_ada = a["w_ada"][0]
    units = [[slice(512 * u, 512 * u + 512), slice(D + 512 * u, D + 512 * u + 512)] for u in range(4)] + \
            [[slice(2 * D + 1024 * w, 2 * D + 1024 * w + 1024)] for w in range(8)]
    ada_of = lambda u, k: np.concatenate([w_ada[tile_of(k), c] for c in units[u]], 1)
    order = [(0, k) for k in range(KT)] + [(u, k) for pair in ADA_PAIRS for k in range(KT) for u in pair] + \
            [(u, k) for u in ADA_SINGLES for k in range(KT)]
    w_ada_s = f(np.stack([ada_of(u, k) for u, k in order]))

    c = np.zeros((32, D), np.float32)
    c[:1], c[1:MODS] = a["c_prompt"], a["c_sample"]
    col = lambda v: v.reshape(-1, P).T
    taps = np.concatenate([a["w_conv"][0], a["b_conv"]], 0).reshape(4, 2 * FT, P).transpose(2, 1, 0).reshape(P, -1)
    vec = np.concatenate([col(a["b_ada"]), col(a["ln1_g"]), col(a["ln1_b"]), col(a["norm_a_g"]), col(a["norm_b_g"]),
                          col(a["ln2_g"]), col(a["ln2_b"]), taps], 1)
    ws = a["w_s"][0]
    bd = np.zeros((NSEQ, TOK, HEADS, NSEQ, TOK), np.float32)
    for n in range(NSEQ):
        bd[n, :, :, n, :] = ws[:, :TOK, :TOK].transpose(2, 0, 1)
    cst, hot = shape_constants()
    n_phys = a["cache_k"].shape[1]
    arrays = {
        "xT": rows_t(a["x_prompt"], a["x_sample"]),
        "cT": f(c.T.reshape(KT, P, 32).transpose(1, 0, 2).reshape(P, -1)),
        "w_ada": w_ada_s, "w_in": w_in_s, "w_out": w_out_s, "w_up": w_up_s, "w_up_tail": w_up_tail,
        "w_down": w_down_s, "w_down_tail": w_down_tail,
        "vec": f(vec), "cst": cst, "hot": hot,
        "rbias": f(np.concatenate([a["rel_bias"], np.full((1, HEADS), NEG, np.float32)], 0)),
        "wsT": f(ws.transpose(2, 0, 1).reshape(P, -1)), "bd": f(bd.reshape(SAMP, -1)),
        "sgu_g": f(a["ln_sgu_g"]), "sgu_b": f(a["ln_sgu_b"]), "b_s": f(a["b_s"].reshape(1, -1)),
        "past": f(a["state_ffn_conv"][0].reshape(NSEQ, 2, 2 * FT, P).transpose(3, 2, 0, 1).reshape(P, -1)),
        "pages": f(a["page_table"].reshape(1, -1)),
        "keys": f(a["cache_k"][0].transpose(0, 3, 2, 1).reshape(n_phys, P, -1)),
        "values": f(a["cache_v"][0].reshape(n_phys, P, -1)),
    }
    outs = {"yT": [P, KT * ROWS], "kvT": [P, 16 * ROWS], "va": [SAMP, 1024], "tails": [P, 2 * FT * 18]}
    nc = bacc.Bacc("TRN2", target_bir_lowering=False, num_devices=1)
    io = {k: nc.dram_tensor(k, v.shape, mybir.dt.from_np(v.dtype), kind="ExternalInput").ap() for k, v in arrays.items()}
    io.update({k: nc.dram_tensor(k, s, F32, kind="ExternalOutput").ap() for k, s in outs.items()})
    decoder_layer_program(nc, io, n_phys)
    r = run_bass_kernel_spmd(nc, [arrays], core_ids=[0]).results[0]

    def rows_of(t, n):
        x = t.reshape(P, n, ROWS).transpose(2, 1, 0).reshape(ROWS, n * P)
        return f(x[:SEQ]), f(x[SEQ:])

    y_p, y_s = rows_of(np.asarray(r["yT"]), KT)
    kv_p, kv_s = rows_of(np.asarray(r["kvT"]), 16)
    tails = np.asarray(r["tails"]).reshape(P, 2 * FT, 18)
    conv_p = f(tails[:, :, :2].transpose(2, 1, 0)).reshape(1, 1, 2, 2 * FF)
    conv_s = f(tails[:, :, 2:].reshape(P, 2 * FT, NSEQ, 2).transpose(2, 3, 1, 0)).reshape(1, NSEQ, 2, 2 * FF)
    half = HEADS * P
    return (y_p.reshape(1, SEQ, D), y_s.reshape(NSEQ, TOK, D),
            f(kv_p[:, :half]).reshape(1, 1, SEQ, HEADS, P), f(kv_p[:, half:]).reshape(1, 1, SEQ, HEADS, P), conv_p,
            f(kv_s[:, :half]).reshape(1, NSEQ, TOK, HEADS, P), f(kv_s[:, half:]).reshape(1, NSEQ, TOK, HEADS, P),
            np.asarray(r["va"]).reshape(1, NSEQ, TOK, 1024), conv_s)
```
